# Optimizing a Trainium2 kernel written in Bass

```python
import jax, jax.numpy as jnp
from jax import lax
import numpy as np

D_MODEL = 2048
BATCH = 1
SEQ = 256
DEPTH = 1

PLE_DIM = 256
GDN_HEADS = 8
GDN_DK = 128
GDN_DV = 128
GDN_CONV = 4
GDN_CHUNK = 64
MOBA_HEADS = 8
MOBA_DH = 128
MOBA_BLOCK = 256
MOBA_TOPK = 3
MOBA_Q_BLOCK = 64
D_FF = -(-8 * D_MODEL // (3 * 256)) * 256
RMS_EPS = 1e-6
GDN_QK_W = GDN_HEADS * GDN_DK
GDN_V_W = GDN_HEADS * GDN_DV
MOBA_W = MOBA_HEADS * MOBA_DH
MIX_W = GDN_V_W + MOBA_W
IN_SPLITS = (GDN_QK_W, GDN_QK_W, GDN_V_W, GDN_V_W, GDN_HEADS, GDN_HEADS, MOBA_W, MOBA_W, MOBA_W)
IN_W = sum(IN_SPLITS)
CONV_W = 2 * GDN_QK_W + GDN_V_W

kernel_name = "hybrid_gdn_moba_parallel_heads"

def rms_norm(x, w, eps=RMS_EPS):
    x32 = x.astype(jnp.float32)
    y = x32 * lax.rsqrt(jnp.mean(x32 * x32, axis=-1, keepdims=True) + eps)
    return (y * w.astype(jnp.float32)).astype(x.dtype)

def l2_norm(x, eps=1e-6):
    return x * lax.rsqrt(jnp.sum(x * x, axis=-1, keepdims=True) + eps)

def causal_short_conv(x, w):
    K = w.shape[1]
    T = x.shape[1]
    xp = jnp.pad(x, ((0, 0), (K - 1, 0), (0, 0)))
    out = xp[:, 0:T] * w[:, 0]
    for j in range(1, K):
        out = out + xp[:, j:j + T] * w[:, j]
    return out

def chunk_gated_delta_rule(q, k, v, g, beta):
    B, T, H, Dk = q.shape
    Dv = v.shape[-1]
    C = GDN_CHUNK
    NC = T // C
    to_chunks = lambda t: t.reshape(B, NC, C, H, t.shape[-1]).transpose(0, 3, 1, 2, 4)
    q, k, v = to_chunks(q), to_chunks(k), to_chunks(v)
    g = g.reshape(B, NC, C, H).transpose(0, 3, 1, 2)
    beta = beta.reshape(B, NC, C, H).transpose(0, 3, 1, 2)
    gc = jnp.cumsum(g, axis=-1)
    tril = jnp.tril(jnp.ones((C, C), dtype=bool))
    strict = jnp.tril(jnp.ones((C, C), dtype=bool), -1)
    decay = jnp.exp(jnp.where(tril, gc[..., :, None] - gc[..., None, :], -jnp.inf))
    k_beta = k * beta[..., None]
    v_beta = v * beta[..., None]
    A = jnp.where(strict, jnp.einsum('bhncd,bhnsd->bhncs', k_beta, k) * decay, 0.0)
    eye = jnp.eye(C, dtype=A.dtype)
    Tm = lax.linalg.triangular_solve(eye + A, jnp.broadcast_to(eye, A.shape),
                                     left_side=True, lower=True)
    u = jnp.einsum('bhncs,bhnse->bhnce', Tm, v_beta)
    w = jnp.einsum('bhncs,bhnsd->bhncd', Tm, k_beta * jnp.exp(gc)[..., None])
    qk = jnp.where(tril, jnp.einsum('bhncd,bhnsd->bhncs', q, k) * decay, 0.0)
    g_last = gc[..., -1]
    k_dec = k * jnp.exp(g_last[..., None] - gc)[..., None]
    q_dec = q * jnp.exp(gc)[..., None]
    xs = tuple(jnp.moveaxis(t, 2, 0) for t in (q_dec, k_dec, u, w, qk, g_last))

    def step(S, inp):
        q_c, k_c, u_c, w_c, qk_c, gl = inp
        v_new = u_c - jnp.einsum('bhcd,bhde->bhce', w_c, S)
        o_c = jnp.einsum('bhcd,bhde->bhce', q_c, S) + jnp.einsum('bhcs,bhse->bhce', qk_c, v_new)
        S = S * jnp.exp(gl)[..., None, None] + jnp.einsum('bhcd,bhce->bhde', k_c, v_new)
        return S, o_c

    S0 = jnp.zeros((B, H, Dk, Dv), jnp.float32)
    _, o = lax.scan(step, S0, xs)
    return o.transpose(1, 0, 3, 2, 4).reshape(B, T, H, Dv)

def gated_deltanet(q, k, v, z, b, a, conv_w, A_log, dt_bias, norm_w):
    B, T, _ = q.shape
    dtype = q.dtype
    qkv = jax.nn.silu(causal_short_conv(jnp.concatenate([q, k, v], axis=-1), conv_w))
    q, k, v = jnp.split(qkv, [GDN_QK_W, 2 * GDN_QK_W], axis=-1)
    q = l2_norm(q.reshape(B, T, GDN_HEADS, GDN_DK).astype(jnp.float32)) * (GDN_DK ** -0.5)
    k = l2_norm(k.reshape(B, T, GDN_HEADS, GDN_DK).astype(jnp.float32))
    v = v.reshape(B, T, GDN_HEADS, GDN_DV).astype(jnp.float32)
    beta = jax.nn.sigmoid(b.astype(jnp.float32))
    g = -jnp.exp(A_log.astype(jnp.float32)) * jax.nn.softplus(a.astype(jnp.float32) + dt_bias.astype(jnp.float32))
    o = chunk_gated_delta_rule(q, k, v, g, beta)
    zh = z.reshape(B, T, GDN_HEADS, GDN_DV).astype(jnp.float32)
    o = rms_norm(o, norm_w) * jax.nn.silu(zh)
    return o.reshape(B, T, GDN_V_W).astype(dtype)

def moba_attention(q, k, v, q_gain, k_gain):
    B, T, _ = q.shape
    H, D, BLK, QB = MOBA_HEADS, MOBA_DH, MOBA_BLOCK, MOBA_Q_BLOCK
    heads = lambda t: t.reshape(B, T, H, D)
    q = rms_norm(heads(q), q_gain)
    k = rms_norm(heads(k), k_gain)
    v = heads(v)
    Tp = -(-T // BLK) * BLK
    pad = ((0, 0), (0, Tp - T), (0, 0), (0, 0))
    q, k, v = [jnp.pad(t, pad).transpose(0, 2, 1, 3) for t in (q, k, v)]
    NB = Tp // BLK
    kb = k.reshape(B, H, NB, BLK, D)
    vb = v.reshape(B, H, NB, BLK, D)
    k_mean = jnp.mean(kb.astype(jnp.float32), axis=3)
    q_blk = jnp.arange(Tp) // BLK
    gate = jnp.einsum('bhtd,bhnd->bhtn', q.astype(jnp.float32), k_mean)
    past = jnp.arange(NB)[None, :] < q_blk[:, None]
    gate = jnp.where(past, gate, -jnp.inf)
    n_sel = min(MOBA_TOPK, NB)
    _, sel = lax.top_k(gate, n_sel)
    valid = sel < q_blk[:, None]
    NQ = Tp // QB
    q_s = q.reshape(B, H, NQ, QB, D).transpose(2, 0, 1, 3, 4)
    sel_s = sel.reshape(B, H, NQ, QB, n_sel).transpose(2, 0, 1, 3, 4)
    valid_s = valid.reshape(B, H, NQ, QB, n_sel).transpose(2, 0, 1, 3, 4)
    b_ix = jnp.arange(B)[:, None, None, None]
    h_ix = jnp.arange(H)[None, :, None, None]
    scale = D ** -0.5

    def query_block(args):
        qi, q_c, sel_c, valid_c = args
        q0 = qi * QB
        own = q0 // BLK
        k_own = lax.dynamic_index_in_dim(kb, own, axis=2, keepdims=False)
        v_own = lax.dynamic_index_in_dim(vb, own, axis=2, keepdims=False)
        k_sel = kb[b_ix, h_ix, sel_c]
        v_sel = vb[b_ix, h_ix, sel_c]
        s_sel = jnp.einsum('bhqd,bhqnkd->bhqnk', q_c, k_sel, preferred_element_type=jnp.float32) * scale
        s_sel = jnp.where(valid_c[..., None], s_sel, -jnp.inf).reshape(B, H, QB, n_sel * BLK)
        s_own = jnp.einsum('bhqd,bhkd->bhqk', q_c, k_own, preferred_element_type=jnp.float32) * scale
        causal = (own * BLK + jnp.arange(BLK))[None, :] <= (q0 + jnp.arange(QB))[:, None]
        s_own = jnp.where(causal, s_own, -jnp.inf)
        probs = jax.nn.softmax(jnp.concatenate([s_sel, s_own], axis=-1), axis=-1).astype(v.dtype)
        p_sel = probs[..., :n_sel * BLK].reshape(B, H, QB, n_sel, BLK)
        p_own = probs[..., n_sel * BLK:]
        return (jnp.einsum('bhqnk,bhqnkd->bhqd', p_sel, v_sel)
                + jnp.einsum('bhqk,bhkd->bhqd', p_own, v_own))

    o = lax.map(query_block, (jnp.arange(NQ), q_s, sel_s, valid_s))
    o = o.transpose(1, 0, 3, 2, 4).reshape(B, Tp, H * D)
    return o[:, :T]

def setup_inputs(seed: int = 0) -> dict:
    key = jax.random.key(seed)
    ks = jax.random.split(key, 20)
    f32 = jnp.float32
    nrm = lambda k, shape, s: jax.random.normal(k, shape, f32) * s
    gain = lambda k, shape: 1.0 + 0.02 * jax.random.normal(k, shape, f32)
    dt = jnp.exp(jax.random.uniform(ks[6], (DEPTH, GDN_HEADS), f32, np.log(1e-3), np.log(1e-1)))
    return {
        "x": jax.random.normal(ks[0], (BATCH, SEQ, D_MODEL), f32),
        "p": jax.random.normal(ks[1], (DEPTH, BATCH, SEQ, PLE_DIM), f32),
        "attn_norm": gain(ks[2], (DEPTH, D_MODEL)),
        "w_in": nrm(ks[3], (DEPTH, D_MODEL, IN_W), D_MODEL ** -0.5),
        "conv_w": nrm(ks[4], (DEPTH, CONV_W, GDN_CONV), GDN_CONV ** -0.5),
        "A_log": jnp.log(jax.random.uniform(ks[5], (DEPTH, GDN_HEADS), f32, 1.0, 16.0)),
        "dt_bias": dt + jnp.log(-jnp.expm1(-dt)),
        "gdn_norm": gain(ks[7], (DEPTH, GDN_DV)),
        "q_norm": gain(ks[8], (DEPTH, MOBA_DH)),
        "k_norm": gain(ks[9], (DEPTH, MOBA_DH)),
        "w_o": nrm(ks[10], (DEPTH, MIX_W, D_MODEL), MIX_W ** -0.5),
        "ffn_norm": gain(ks[11], (DEPTH, D_MODEL)),
        "w_gate": nrm(ks[12], (DEPTH, D_MODEL, D_FF), D_MODEL ** -0.5),
        "w_up": nrm(ks[13], (DEPTH, D_MODEL, D_FF), D_MODEL ** -0.5),
        "w_down": nrm(ks[14], (DEPTH, D_FF, D_MODEL), D_FF ** -0.5),
        "ple_norm": gain(ks[15], (DEPTH, D_MODEL)),
        "w_ple_gate": nrm(ks[16], (DEPTH, D_MODEL, D_MODEL), D_MODEL ** -0.5),
        "w_ple_proj": nrm(ks[17], (DEPTH, PLE_DIM, D_MODEL), PLE_DIM ** -0.5),
    }

def reference(x, p, attn_norm, w_in, conv_w, A_log, dt_bias, gdn_norm, q_norm, k_norm,
              w_o, ffn_norm, w_gate, w_up, w_down, ple_norm, w_ple_gate, w_ple_proj):
    h = x
    split_at = list(np.cumsum(IN_SPLITS)[:-1])
    for i in range(DEPTH):
        xn = rms_norm(h, attn_norm[i])
        proj = xn @ w_in[i]
        gq, gk, gv, gz, gb, ga, mq, mk, mv = jnp.split(proj, split_at, axis=-1)
        o_gdn = gated_deltanet(gq, gk, gv, gz, gb, ga, conv_w[i], A_log[i], dt_bias[i], gdn_norm[i])
        o_moba = moba_attention(mq, mk, mv, q_norm[i], k_norm[i])
        h = h + jnp.concatenate([o_gdn, o_moba], axis=-1) @ w_o[i]
        hn = rms_norm(h, ffn_norm[i])
        h = h + (jax.nn.silu(hn @ w_gate[i]) * (hn @ w_up[i])) @ w_down[i]
        gate = jax.nn.sigmoid(rms_norm(h, ple_norm[i]) @ w_ple_gate[i])
        h = h + gate * (p[i] @ w_ple_proj[i])
    return h


_drawn_inputs = setup_inputs


def setup_inputs(seed=0):
    import zlib

    import numpy as np

    out = dict(_drawn_inputs(seed))
    spreads = {}
    factors = {'attn_norm': 4.014,
     'gdn_norm': 7.059,
     'q_norm': 8.0,
     'k_norm': 8.0,
     'ffn_norm': 12.793,
     'ple_norm': 200.0,
     'p': 8.0,
     'w_ple_gate': 8.0,
     'w_ple_proj': 8.0}
    for name, (base, spread) in spreads.items():
        noise = np.random.default_rng([zlib.crc32(name.encode()), seed]).standard_normal(out[name].shape)
        drawn = base * np.exp(spread * noise) if base else spread * noise
        out[name] = __import__('jax').numpy.asarray(drawn.astype(out[name].dtype))
    for name, factor in factors.items():
        out[name] = (out[name] * factor).astype(out[name].dtype)
    return out
```

```python
from contextlib import ExitStack

import concourse.bass as bass
from concourse import mybir

ALU = mybir.AluOpType
ACT = mybir.ActivationFunctionType
AX_X = mybir.AxisListType.X
F32 = mybir.dt.float32
F32R = mybir.dt.float32r

P = 128
TOK = 256
NT = TOK // P
D = 2048
KT = D // P
CB = 512
FF = 5632
HEADS = 8
HG = 4
PLE = 256
CONV = 4
EPS = 1e-6
BANKS = 4
RING = 4
KU = 2
LEAD = 3
CHAN = 3 * HEADS
C_Z, C_BA, C_MOBA = 3 * HEADS * P, 4 * HEADS * P, 4 * HEADS * P + 2 * HEADS
LEVELS = 7
NEG = -1e30

UPB = KT // KU
U_QKV, B_QKV = 0, 0
U_MIX, B_MIX = 6 * UPB, 6
U_WO, B_WO = U_MIX + 8 * UPB, 14
U_PP, B_PP = U_WO + 4 * UPB, 18
FF_A, FF_B = 6, 5
U_GUA, B_GUA = U_PP + 4, 22
U_DA, B_DA = U_GUA + FF_A * 2 * UPB, 22 + 2 * FF_A
U_GUB, B_GUB = U_DA + 4 * (FF_A * 4 // KU), B_DA + 4
U_DB, B_DB = U_GUB + FF_B * 2 * UPB, B_GUB + 2 * FF_B
U_PG, B_PG = U_DB + 4 * (FF_B * 4 // KU), B_DB + 4
UNITS = U_PG + 4 * UPB
assert not any(u % RING for u in (U_MIX, U_WO, U_PP, U_GUA, U_DA, U_GUB, U_DB, U_PG))


def chunk_steps(b):
    steps = ["q_tok", "k_tok", "v_tok", "qT", "kT", "kbT", "gcrow", "gramQ", "gramA", "T0"]
    for l in range(1, LEVELS - 1):
        steps += [f"Y{l}", f"Z{l}", f"TT{l}"]
    steps += [f"Y{LEVELS - 1}", "ZT"]
    steps += ["ks", "u", "qs", "o", "ogT"] if b % 2 else ["u", "S", "o", "ogT"]
    return [(s, b) for s in steps]


def plan():
    first = [("gains", 0)] + [("x", g) for g in range(KT // 2)] + [("p", 0)]
    gates = [("ba", 0), ("gc", 0)]
    delta = []
    for hg in range(HEADS // HG):
        even, odd = chunk_steps(2 * hg), chunk_steps(2 * hg + 1)
        lag = 3
        for i in range(len(odd) + lag):
            delta += even[i:i + 1] + (odd[i - lag:i - lag + 1] if i >= lag else [])
    at = {u: [[], []] for u in range(UNITS)}
    slots = [(u, k) for u in range(U_MIX, U_WO) for k in range(2)]
    for n, s in enumerate(delta):
        u, k = slots[n * 2 // 3]
        at[u][k].append(s)
    for j in range(4):
        for t in range(NT):
            at[U_MIX + (3 + j) * UPB + 3 + 2 * t][1].append(("mT", 2 * j + t))
    v0 = U_MIX + 6 * UPB + 6
    for h in range(HEADS):
        at[v0 + h][0].append(("sc", h))
        at[v0 + h + 1][1].append(("pT", h))
    for h in range(HEADS):
        at[U_WO + h // 2][h % 2].append(("pv", h))
    for n in range(4):
        for g in range(2):
            at[(U_WO + (n + 1) * UPB if n < 3 else U_PP) + 2][g].append(("hA", 2 * n + g))
            at[(U_DB + (n + 1) * (FF_B * 4 // KU) if n < 3 else U_PG) + 3][g].append(("hB", 2 * n + g))
    order = first + gates + [s for u in range(UNITS) for k in at[u] for s in k]
    return first, gates, at, {s: n for n, s in enumerate(order)}


def build(nc, A):
    FIRST, GATES, AT, NUMBER = plan()

    with ExitStack() as ctx:
        place = [16512]

        def sb(name, shape, dtype=F32, at=None):
            size = 4
            for n in shape[1:]:
                size *= n
            where = place[0] if at is None else at
            if at is None:
                place[0] += (size + 31) // 32 * 32
            return nc.alloc_sbuf_tensor_at(name, shape, dtype, offset=where)

        def sem(name):
            return ctx.enter_context(nc.semaphore(name))

        def bank(name):
            return ctx.enter_context(nc.psum_tensor(name, [P, CB], F32))

        xT_hi = sb("xT_hi", [P, KT, TOK], F32R)
        xT_lo = sb("xT_lo", [P, KT, TOK], F32R)
        raw = [sb(f"raw{i}", [P, KU, CB]) for i in range(RING)]
        w_hi = [sb(f"w_hi{i}", [P, KU, CB], F32R) for i in range(RING)]
        w_lo = [sb(f"w_lo{i}", [P, KU, CB], F32R) for i in range(RING)]
        mix = place[0]
        KIB = 1024
        place[0] += 64 * KIB
        ch = sb("ch", [P, CHAN, TOK], at=mix)
        og_hi = sb("og_hi", [P, HEADS, TOK], F32R, at=mix)
        og_lo = sb("og_lo", [P, HEADS, TOK], F32R, at=mix + 8 * KIB)
        om_hi = sb("om_hi", [P, HEADS, TOK], F32R, at=mix + 24 * KIB)
        om_lo = sb("om_lo", [P, HEADS, TOK], F32R, at=mix + 32 * KIB)
        names = ("AT", "T", "TT", "Y", "V", "KD")
        G = [{n: sb(f"{n}{c}", [P, HG, P], at=mix + (40 + 12 * c + 2 * i) * KIB) for i, n in enumerate(names)}
             for c in range(2)]
        actT_hi = sb("actT_hi", [P, 4 * FF_A, TOK], F32R, at=mix)
        actT_lo = sb("actT_lo", [P, 4 * FF_A, TOK], F32R, at=mix + 24 * KIB)
        gate_s = [sb(f"gate_s{t}", [P, CB], at=mix + (48 + 2 * t) * KIB) for t in range(NT)]
        act_s = [sb(f"act_s{t}", [P, CB], at=mix + (52 + 2 * t) * KIB) for t in range(NT)]
        junk = sb("junk", [P, CB], at=mix + 56 * KIB)
        x_junk = sb("x_junk", [P, D], at=mix)
        wba_raw = sb("wba_raw", [P, KT, 2 * HEADS], at=mix + 24 * KIB)
        wba_hi = sb("wba_hi", [P, KT, 2 * HEADS], F32R, at=mix + 25 * KIB)
        wba_lo = sb("wba_lo", [P, KT, 2 * HEADS], F32R, at=mix + 26 * KIB)
        res = place[0]
        place[0] += 32 * KIB
        h = sb("h", [P, NT, D], at=res)
        mv = sb("mv", [P, NT, HEADS * P], at=res)
        zg = sb("zg", [P, NT, HEADS * P], at=res + 8 * KIB)
        mT = [sb("mqT", [P, HEADS, TOK], at=res + 16 * KIB), sb("mkT", [P, HEADS, TOK], at=res + 24 * KIB)]
        pp = sb("pp", [P, NT, D], at=res + 16 * KIB)
        sq = [sb(f"sq{t}", [P, CB]) for t in range(NT)]
        mn = [sb(f"mn{t}", [P, CB]) for t in range(NT)]
        state = sb("state", [P, HG, P])
        pr = [sb(f"pr{i}", [P, 3 * P]) for i in range(2)]
        prT = [sb(f"prT{i}", [P, 3 * P], at=mix + 40 * KIB + i * 3 * P * 4) for i in range(HEADS)]
        p_in = sb("p_in", [P, NT, PLE])
        pT_hi = sb("pT_hi", [P, PLE // P, TOK], F32R)
        pT_lo = sb("pT_lo", [P, PLE // P, TOK], F32R)
        ident = sb("ident", [P, P])
        triu = sb("triu", [P, P])
        ones = sb("ones", [P, P])
        join = sb("join", [P, LEVELS, P])
        join0T = sb("join0T", [P, P])
        causal = sb("causal", [P, 3 * P])
        NROW = 3 * KT + 3
        rows = sb("rows", [NROW, P])
        gains = sb("gains", [P, NROW + 1])
        G_ATTN, G_FFN, G_PLE, G_GDN, G_Q, G_K, G_QS = 0, KT, 2 * KT, 3 * KT, 3 * KT + 1, 3 * KT + 2, 3 * KT + 3
        convw = sb("convw", [P, CHAN * CONV])
        a_log = sb("a_log", [P, HEADS])
        dt_b = sb("dt_b", [P, HEADS])
        exp_a = sb("exp_a", [P, HEADS])
        sc = {n: sb(n, [P, NT, HEADS]) for n in ("beta", "dt_in", "dt_abs", "dt_exp", "dt_ln", "dt_sum", "g", "gc", "egc")}
        half = sb("half", [P, 2 * HEADS])
        x_ss, x_ms, x_rs = (sb(n, [P, NT]) for n in ("x_ss", "x_ms", "x_rs"))
        q_ss, q_ms, q_rs, k_ss, k_ms, k_rs, o_ss, o_ms, o_rs = (
            [sb(f"{n}{c}", [P, HG]) for c in range(2)]
            for n in ("q_ss", "q_ms", "q_rs", "k_ss", "k_ms", "k_rs", "o_ss", "o_ms", "o_rs"))
        m_ss, m_ms, m_rs = ([sb(f"{n}{t}", [P, HG]) for t in range(NT)] for n in ("m_ss", "m_ms", "m_rs"))
        nmax, psum_p, rsum = ([sb(f"{n}{i}", [P, 2]) for i in range(2)] for n in ("nmax", "psum_p", "rsum"))
        h_ss = [sb(f"h_ss{i}", [P, NT, 4]) for i in range(2)]
        h_s, h_ms, h_rs = ([sb(f"{n}{i}", [P, NT]) for i in range(2)] for n in ("h_s", "h_ms", "h_rs"))

        pair = [[bank(f"pair{i}{t}") for t in range(2)] for i in range(2)]
        bg = [bank(f"bg{i}") for i in range(BANKS)]

        raw_landed = [sem(f"raw_landed{i}") for i in range(RING)]
        hi_ready, lo_ready, unit_used = sem("hi_ready"), sem("lo_ready"), sem("unit_used")
        pair_free = [sem("pair_free0"), sem("pair_free1")]
        bank_full = [sem(f"bank_full{i}") for i in range(BANKS)]
        bank_free = [sem(f"bank_free{i}") for i in range(BANKS)]
        x_landed, x_again, p_landed = [sem("x_landed0"), sem("x_landed1")], sem("x_again"), sem("p_landed")
        small_landed, rows_landed, ba_landed = sem("small_landed"), sem("rows_landed"), sem("ba_landed")
        masks_ready, consts_ready, out_landed = sem("masks_ready"), sem("consts_ready"), sem("out_landed")
        x_sq, x_mean, x_rstd, x_scaled = sem("x_sq"), sem("x_mean"), sem("x_rstd"), sem("x_scaled")
        gain_s, x_hi, p_hi, ba_hi, ba_lo = sem("gain_s"), sem("x_hi"), sem("p_hi"), sem("ba_hi"), sem("ba_lo")
        tap3, taps, conv_sig = sem("tap3"), sem("taps"), sem("conv_sig")
        beta_ready, dt_dve, dt_act, g_ready, egc_ready = (
            sem(n) for n in ("beta_ready", "dt_dve", "dt_act", "g_ready", "egc_ready"))
        q_sq, q_sum, q_rstd, k_sq, k_sum, k_rstd, kb_ready = (
            sem(n) for n in ("q_sq", "q_sum", "q_rstd", "k_sq", "k_sum", "k_rstd", "kb_ready"))
        gtri_ready, gap_ready, exp_ready, decay_ready, kd_ready, tt_mid = (
            sem(n) for n in ("gtri_ready", "gap_ready", "exp_ready", "decay_ready", "kd_ready", "tt_mid"))
        tt0, r_ready, o_sq, o_sum, o_rstd, o_scaled, og_ready, og_hi_ready = (
            sem(n) for n in ("tt0", "r_ready", "o_sq", "o_sum", "o_rstd", "o_scaled", "og_ready", "og_hi_ready"))
        z_sig, m_sq, m_sum, m_rstd, mn_ready = (sem(n) for n in ("z_sig", "m_sq", "m_sum", "m_rstd", "mn_ready"))
        max_ready, exp_done, rsum_ready, p_ready, om_hi_ready = (
            sem(n) for n in ("max_ready", "exp_done", "rsum_ready", "p_ready", "om_hi_ready"))
        h_sq, h_sum, h_rstd, h_hi = sem("h_sq"), sem("h_sum"), sem("h_rstd"), sem("h_hi")
        gate_sig, act_hi_ready = sem("gate_sig"), sem("act_hi_ready")
        ff_full, ff_free = [sem("ff_full0"), sem("ff_full1")], [sem("ff_free0"), sem("ff_free1")]
        pg_mul, out_ready = sem("pg_mul"), sem("out_ready")

        def where(step):
            n = NUMBER[step]
            return bg[n % BANKS], n % BANKS, n // BANKS

        def wait_full(eng, step):
            _, i, use = where(step)
            eng.wait_ge(bank_full[i], use + 1)

        def wait_read(eng, step):
            _, i, use = where(step)
            eng.wait_ge(bank_free[i], use + 1)

        def read_out(step, instruction):
            instruction.then_inc(bank_free[where(step)[1]], 1)

        def heads(ap):
            return ap.rearrange("p (h n) -> p h n", h=HG)

        def over_cols(ap):
            return ap.unsqueeze(2).to_broadcast([P, HG, P])

        def over_heads(ap):
            return ap.unsqueeze(1).to_broadcast([P, HG, P])

        def wait_block(eng, last_unit):
            eng.wait_ge(unit_used, last_unit + 1)

        def wait_pair_read(eng, block):
            eng.wait_ge(pair_free[block % 2], 2 * (block // 2 + 1))

        w_in = A["w_in"][0].rearrange("(k p) n -> p k n", p=P)
        w_o = A["w_o"][0].rearrange("(k p) n -> p k n", p=P)
        w_gate = A["w_gate"][0].rearrange("(k p) n -> p k n", p=P)
        w_up = A["w_up"][0].rearrange("(k p) n -> p k n", p=P)
        w_down = A["w_down"][0].rearrange("(k p) n -> p k n", p=P)
        w_pg = A["w_ple_gate"][0].rearrange("(k p) n -> p k n", p=P)
        w_pp = A["w_ple_proj"][0].rearrange("(k p) n -> p k n", p=P)
        x_d = A["x"][0].rearrange("(t p) n -> p t n", p=P)
        out_d = A["out"][0].rearrange("(t p) n -> p t n", p=P)

        block = ctx.enter_context(nc.Block())

        @block.sync
        def _(sp):
            def load(u, j, w, k, col):
                if not isinstance(u, int) or u >= RING:
                    sp.wait_ge(lo_ready, u - (RING - 1))
                sp.dma_start(raw[j % RING][:], w[:, k:k + KU, bass.ds(col, CB)]).then_inc(raw_landed[j % RING], 16)

            for t in range(NT):
                sp.dma_start(h[:, t, :], x_d[:, t, :]).then_inc(x_landed[t], 16)
            for j in range(2 * UPB):
                load(j, j, w_in, KU * (j % UPB), j // UPB * CB)
            with sp.Fori(1, 3) as i:
                for j in range(2 * UPB):
                    load(i * (2 * UPB) + j, j, w_in, KU * (j % UPB), i * (2 * CB) + j // UPB * CB)
            for b in range(8):
                col = C_Z + b * CB if b < 2 else C_MOBA + (b - 2) * CB
                for j in range(UPB):
                    load(U_MIX + b * UPB + j, j, w_in, KU * j, col)
            for b in range(4):
                if b == 1:
                    wait_read(sp, ("pv", HEADS - 1))
                    wait_read(sp, ("ogT", 3))
                    wait_read(sp, ("ogT", 2))
                    sp.dma_start(h[:], x_d).then_inc(x_again, 16)
                for j in range(UPB):
                    load(U_WO + b * UPB + j, j, w_o, KU * j, b * CB)
            for b in range(4):
                load(U_PP + b, b, w_pp, 0, b * CB)
            for u0, u1, n, at in ((U_GUA, U_DA, FF_A, 0), (U_GUB, U_DB, FF_B, FF_A)):
                with sp.Fori(0, n) as i:
                    for j in range(2 * UPB):
                        w = w_gate if j < UPB else w_up
                        load(i * (2 * UPB) + (u0 + j), j, w, KU * (j % UPB), i * CB + at * CB)
                per = n * 4 // KU
                with sp.Fori(0, 2) as i:
                    for j in range(2 * per):
                        load(i * (2 * per) + (u1 + j), j, w_down, at * 4 + KU * (j % per),
                             i * (2 * CB) + j // per * CB)
            with sp.Fori(0, 2) as i:
                for j in range(2 * UPB):
                    load(i * (2 * UPB) + (U_PG + j), j, w_pg, KU * (j % UPB), i * (2 * CB) + j // UPB * CB)
            for b in range(4):
                sp.wait_ge(out_ready, 2 * (b + 1))
                sp.dma_start(out_d[:, :, b * CB:(b + 1) * CB], h[:, :, b * CB:(b + 1) * CB]).then_inc(out_landed, 16)
            sp.wait_ge(out_landed, 64)

        @block.gpsimd
        def _(pool):
            g = nc.gpsimd
            n = 0

            def mask(ins):
                nonlocal n
                n += 1
                ins.then_inc(masks_ready, 1)
                pool.wait_ge(masks_ready, n)

            mask(g.memset(half[:], -0.5))
            mask(g.memset(ones[:], 1.0))
            mask(g.memset(ident[:], 0.0))
            mask(g.affine_select(out=ident[:], in_=ident[:], compare_op=ALU.not_equal, fill=1.0, base=0,
                                 pattern=[[-1, P]], channel_multiplier=1))
            mask(g.affine_select(out=triu[:], in_=ones[:], compare_op=ALU.is_ge, fill=0.0, base=0,
                                 pattern=[[1, P]], channel_multiplier=-1))
            mask(g.memset(causal[:], 0.0))
            for o in (0, 2 * P):
                mask(g.affine_select(out=causal[:, o:o + P], in_=causal[:, o:o + P], compare_op=ALU.is_ge, fill=NEG,
                                     base=0, pattern=[[-1, P]], channel_multiplier=1))
            mask(g.memset(join[:], 0.0))
            for l in range(LEVELS):
                b = 1 << l
                m = join[:, l, :].rearrange("p (j two b) -> p j two b", two=2, b=b)[:, :, 0, :]
                o = ones[:].rearrange("p (j two b) -> p j two b", two=2, b=b)[:, :, 0, :]
                mask(g.affine_select(out=m, in_=o, compare_op=ALU.is_ge, fill=0.0, base=-b,
                                     pattern=[[-2 * b, P // (2 * b)], [0, b]], channel_multiplier=1))
                mask(g.affine_select(out=m, in_=m, compare_op=ALU.is_ge, fill=0.0, base=2 * b - 1,
                                     pattern=[[2 * b, P // (2 * b)], [0, b]], channel_multiplier=-1))
            mask(g.memset(join0T[:], 0.0))
            m = join0T[:].rearrange("p (j two) -> p j two", two=2)[:, :, 1]
            mask(g.affine_select(out=m, in_=m, compare_op=ALU.not_equal, fill=1.0, base=0,
                                 pattern=[[-2, P // 2]], channel_multiplier=1))
            g.memset(join0T[:, 0:1], 0.0).then_inc(consts_ready, 1)

            def rstd(out, mid, ss, scale, eps, done, count):
                g.tensor_scalar(mid, ss, scale, eps, ALU.mult, ALU.add).then_inc(done, 1)
                pool.wait_ge(done, 2 * count + 1)
                g.tensor_tensor(out, mid, half[:, 0:mid.shape[1]], ALU.pow).then_inc(done, 1)

            pool.wait_ge(x_sq, NT)
            rstd(x_rs[:], x_ms[:], x_ss[:], 1.0 / D, EPS, x_rstd, 0)

            def post(step, b):
                c, hg = b % 2, b // 2
                B = G[c] if step not in ("mT", "sc", "pT", "pv") else None
                hs = slice(HG * hg, HG * hg + HG)
                if step == "q_tok":
                    pool.wait_ge(q_sum, b + 1)
                    rstd(q_rs[c][:], q_ms[c][:], q_ss[c][:], float(P), P * EPS, q_rstd, b)
                elif step == "k_tok":
                    pool.wait_ge(k_sum, b + 1)
                    rstd(k_rs[c][:], k_ms[c][:], k_ss[c][:], 1.0, EPS, k_rstd, b)
                    wait_read(pool, (step, b))
                    g.tensor_tensor(B["TT"][:], B["T"][:], over_cols(sc["beta"][:, c, hs]),
                                    ALU.mult).then_inc(kb_ready, 1)
                elif step == "kbT":
                    wait_full(pool, (step, b))
                    g.tensor_tensor(B["TT"][:], over_heads(triu[:]), over_cols(sc["g"][:, c, hs]),
                                    ALU.mult).then_inc(gtri_ready, 1)
                elif step == "gcrow":
                    pool.wait_ge(exp_ready, b + 1)
                    g.tensor_tensor(B["KD"][:], B["T"][:], B["Y"][:, :, P - 1:P].to_broadcast([P, HG, P]),
                                    ALU.mult).then_inc(kd_ready, 1)
                    pool.wait_ge(kd_ready, b + 1)
                    g.tensor_tensor(B["Y"][:], B["Y"][:], over_heads(triu[:]), ALU.mult).then_inc(decay_ready, 1)
                elif step == "o":
                    pool.wait_ge(o_sum, b + 1)
                    rstd(o_rs[c][:], o_ms[c][:], o_ss[c][:], 1.0 / P, EPS, o_rstd, b)

            def block_end(b):
                if 2 <= b < 6:
                    for t in range(NT):
                        i = 2 * (b - 2) + t
                        pool.wait_ge(m_sum, i + 1)
                        rstd(m_rs[t][:], m_ms[t][:], m_ss[t][:], 1.0 / P, EPS, m_rstd, i)

            pool.wait_ge(g_ready, 1)
            for u in range(U_MIX, U_WO):
                for k in range(2):
                    for s in AT[u][k]:
                        post(*s)
                if (u + 1) % UPB == 0:
                    block_end((u - U_MIX) // UPB)
            for i in range(2):
                pool.wait_ge(h_sum, i + 1)
                rstd(h_rs[i][:], h_ms[i][:], h_s[i][:], 1.0 / D, EPS, h_rstd, i)

        @block.tensor
        def _(pe):
            mm, tp = nc.tensor.matmul, nc.tensor.transpose

            def use(u):
                pe.wait_ge(lo_ready, u + 1)

            def k_tile(j, kk, hi, lo, banks, first, last):
                wh, wl = w_hi[j % RING][:, kk, :], w_lo[j % RING][:, kk, :]
                for t in range(NT):
                    ts = slice(t * P, t * P + P)
                    mm(banks[t][:], hi[:, ts], wh, start=first, stop=False)
                    mm(banks[t][:], hi[:, ts], wl, start=False, stop=False)
                    m = mm(banks[t][:], lo[:, ts], wh, start=False, stop=last)
                return m

            def burst(s):
                step, b = s
                bk, i, use_n = where(s)
                c, hg = b % 2, b // 2
                if use_n:
                    pe.wait_ge(bank_free[i], use_n)
                bh = heads(bk[:])
                last = None
                if step == "gains":
                    pe.wait_ge(rows_landed, 16 * 6)
                    pe.wait_ge(consts_ready, 1)
                    last = tp(bk[:, 0:NROW], rows[:], ident[0:NROW, 0:NROW])
                elif step in ("x", "hA", "hB"):
                    if step == "x":
                        if b == 0:
                            pe.wait_ge(x_scaled, NT)
                    elif b % 2 == 0:
                        block = (B_WO if step == "hA" else B_DB) + b // 2
                        wait_pair_read(pe, block)
                    for kk in range(2):
                        for t in range(NT):
                            k = 2 * b + kk
                            last = tp(bk[:, kk * TOK + t * P:kk * TOK + t * P + P], h[:, t, k * P:(k + 1) * P], ident[:])
                elif step == "p":
                    pe.wait_ge(p_landed, 16)
                    for kk in range(2):
                        for t in range(NT):
                            last = tp(bk[:, kk * TOK + t * P:kk * TOK + t * P + P], p_in[:, t, kk * P:(kk + 1) * P], ident[:])
                elif step == "ba":
                    pe.wait_ge(ba_lo, 1)
                    for t in range(NT):
                        o = bk[:, t * 2 * HEADS:(t + 1) * 2 * HEADS]
                        ts = slice(t * P, t * P + P)
                        for k in range(KT):
                            mm(o, xT_hi[:, k, ts], wba_hi[:, k, :], start=(k == 0), stop=False)
                            mm(o, xT_hi[:, k, ts], wba_lo[:, k, :], start=False, stop=False)
                            last = mm(o, xT_lo[:, k, ts], wba_hi[:, k, :], start=False, stop=(k == KT - 1))
                elif step == "gc":
                    pe.wait_ge(g_ready, 1)
                    for t in range(NT):
                        last = mm(bk[:, t * HEADS:(t + 1) * HEADS], triu[:], sc["g"][:, t, :], start=True, stop=True)
                elif step == "mT":
                    pe.wait_ge(mn_ready, b + 1)
                    for j in range(HG):
                        last = tp(bh[:, j, :], mn[c][:, j * P:(j + 1) * P], ident[:])
                elif step == "sc":
                    for j in (b // HG, 2 + b // HG):
                        for t in range(NT):
                            wait_read(pe, ("mT", 2 * j + t))
                    mm(bk[:, 0:P], mT[0][:, b, 0:P], mT[1][:, b, 0:P], start=True, stop=True)
                    last = mm(bk[:, P:3 * P], mT[0][:, b, P:TOK], mT[1][:, b, :], start=True, stop=True)
                elif step == "pT":
                    if b == 0:
                        for s_ in (2, 3):
                            wait_read(pe, ("ogT", s_))
                    pe.wait_ge(p_ready, b + 1)
                    for j in range(3):
                        last = tp(bk[:, j * P:(j + 1) * P], pr[c][:, j * P:(j + 1) * P], ident[:])
                elif step == "pv":
                    wait_read(pe, ("pT", b))
                    if b == 0:
                        wait_pair_read(pe, B_MIX + 6)
                        wait_pair_read(pe, B_MIX + 7)
                    cs = slice(b * P, b * P + P)
                    mm(bk[:, 0:TOK], mv[:, 0, cs], prT[b][:, 0:TOK], start=True, stop=False, skip_group_check=True)
                    last = mm(bk[:, P:TOK], mv[:, 1, cs], prT[b][:, TOK:3 * P], start=False, stop=True,
                              skip_group_check=True)
                else:
                    last = delta(step, b, bh, G[c], c, hg)
                last.then_inc(bank_full[i], 1)

            def delta(step, b, bh, B, c, hg):
                ts = slice(c * P, c * P + P)
                last = None
                prev = {s: p for p, s in zip([x[0] for x in chunk_steps(b)], [x[0] for x in chunk_steps(b)][1:])}.get(step)
                if step == "q_tok":
                    if b < 2:
                        for q in range(2):
                            wait_pair_read(pe, B_MIX - 2 + q)
                    else:
                        wait_read(pe, ("ogT", b - 2))
                elif step == "k_tok" or step == "v_tok":
                    pass
                elif step == "qT":
                    wait_read(pe, ("q_tok", b))
                elif step == "kT":
                    wait_read(pe, ("k_tok", b))
                elif step == "kbT":
                    pe.wait_ge(kb_ready, b + 1)
                elif step == "gcrow":
                    pe.wait_ge(gtri_ready, b + 1)
                elif step == "gramQ":
                    for s in ("qT", "kT", "kbT"):
                        wait_read(pe, (s, b))
                elif step == "gramA":
                    pass
                elif step == "T0":
                    pe.wait_ge(tt0, b + 1)
                elif step == "ks":
                    wait_read(pe, (prev, b))
                    wait_read(pe, ("S", b - 1))
                elif step == "u" and c:
                    pe.wait_ge(r_ready, (b + 1) // 2)
                elif step == "qs":
                    pass
                elif step == "S":
                    wait_read(pe, ("u", b))
                    pe.wait_ge(kd_ready, b + 1)
                elif step == "o":
                    wait_read(pe, ("u", b))
                    wait_read(pe, ("gramQ", b))
                elif step == "ogT":
                    pe.wait_ge(og_ready, b + 1)
                else:
                    wait_read(pe, (prev, b))
                for j in range(HG):
                    hd = HG * hg + j
                    o = bh[:, j, :]
                    if step in ("q_tok", "k_tok", "v_tok"):
                        base = {"q_tok": 0, "k_tok": HEADS, "v_tok": 2 * HEADS}[step]
                        last = tp(o, ch[:, base + hd, ts], ident[:])
                    elif step in ("qT", "kT", "kbT", "T0", "ogT") or step.startswith("TT"):
                        src = {"qT": "Y", "kT": "T", "kbT": "TT", "T0": "TT", "ogT": "V"}.get(step, "T")
                        last = tp(o, B[src][:, j, :], ident[:])
                    elif step == "gcrow":
                        last = mm(o, ones[:], B["TT"][:, j, :], start=True, stop=True)
                    else:
                        l, r = {
                            "gramQ": lambda: (B["AT"][:, j, :], ch[:, hd, ts]),
                            "gramA": lambda: (B["AT"][:, j, :], ch[:, HEADS + hd, ts]),
                            "Y": lambda: (B["AT"][:, j, :], B["T"][:, j, :]),
                            "Z": lambda: (B["TT"][:, j, :], B["Y"][:, j, :]),
                            "ZT": lambda: (B["Y"][:, j, :], B["TT"][:, j, :]),
                            "ks": lambda: (ch[:, HEADS + hd, ts], state[:, j, :]),
                            "qs": lambda: (ch[:, hd, ts], state[:, j, :]),
                            "u": lambda: (B["TT"][:, j, :], B["V"][:, j, :]),
                            "S": lambda: (B["KD"][:, j, :], B["T"][:, j, :]),
                            "o": lambda: (ch[:, 2 * HEADS + hd, ts], B["T"][:, j, :]),
                        }[step if step in ("gramQ", "gramA", "ZT", "ks", "qs", "u", "S", "o") else step[0]]()
                        last = mm(o, l, r, start=True, stop=True)
                return last

            for s in FIRST:
                burst(s)
            wait_read(pe, ("x", KT // 2 - 1))
            wait_read(pe, ("x", KT // 2 - 2))
            wait_read(pe, ("x", KT // 2 - 3))
            wait_read(pe, ("x", KT // 2 - 4))

            def qkv(i, first):
                for j in range(2 * UPB):
                    use(i * (2 * UPB) + j)
                    bl = j // UPB
                    if j % UPB == 0 and not first:
                        pe.wait_ge(pair_free[bl], i * 2)
                    for kk in range(KU):
                        k = KU * (j % UPB) + kk
                        for m in range(4):
                            o = pair[bl][m // 2][:, m % 2 * TOK:(m % 2 + 1) * TOK]
                            ms = slice(m * P, m * P + P)
                            wh, wl = w_hi[j % RING][:, kk, ms], w_lo[j % RING][:, kk, ms]
                            mm(o, wh, xT_hi[:, k, :], start=(k == 0 and m % 2 == 0), stop=False, skip_group_check=True)
                            mm(o, wh, xT_lo[:, k, :], start=False, stop=False, skip_group_check=True)
                            last = mm(o, wl, xT_hi[:, k, :], start=False, stop=(k == KT - 1 and m % 2 == 1),
                                      skip_group_check=True)
                    last.then_inc(unit_used, 1)

            qkv(0, True)
            with pe.Fori(1, 3) as i:
                qkv(i, False)
            for s in GATES:
                burst(s)

            def straight(u0, b0, blocks, per, hi_lo):
                for b in range(blocks):
                    pe.wait_ge(pair_free[(b0 + b) % 2], 2 * ((b0 + b) // 2))
                    for j in range(per):
                        u = u0 + b * per + j
                        use(u)
                        for kk in range(KU):
                            k = KU * j + kk
                            hi, lo = hi_lo(b, k)
                            last = k_tile(u, kk, hi, lo, pair[(b0 + b) % 2], k == 0, k == KU * per - 1)
                            if kk == KU - 1:
                                last.then_inc(unit_used, 1)
                            for s in AT[u][kk]:
                                burst(s)

            straight(U_MIX, B_MIX, 8, UPB, lambda b, k: (xT_hi[:, k, :], xT_lo[:, k, :]))

            def mixed(b, k):
                if b == 0 and k == 0:
                    for s in range(4):
                        wait_read(pe, ("ogT", s))
                if b == 0 and k == HEADS:
                    for s in range(HEADS):
                        wait_read(pe, ("pv", s))
                if k < HEADS:
                    return og_hi[:, k, :], og_lo[:, k, :]
                return om_hi[:, k - HEADS, :], om_lo[:, k - HEADS, :]

            straight(U_WO, B_WO, 4, UPB, mixed)
            straight(U_PP, B_PP, 4, 1, lambda b, k: (pT_hi[:, k, :], pT_lo[:, k, :]))

            def turn_act():
                for q in range(2):
                    for kk in range(2):
                        for t in range(NT):
                            cs = slice((2 * q + kk) * P, (2 * q + kk + 1) * P)
                            m = tp(bg[q][:, kk * TOK + t * P:kk * TOK + t * P + P], act_s[t][:, cs], ident[:])
                    m.then_inc(ff_full[q], 1)

            def gate_up(i, u0, b0, n0, peeled):
                for j in range(2 * UPB):
                    use(i * (2 * UPB) + (u0 + j))
                    bl = j // UPB
                    if j % UPB == 0:
                        pe.wait_ge(pair_free[bl], i * 2 + b0)
                    for kk in range(KU):
                        k = KU * (j % UPB) + kk
                        last = k_tile(j, kk, xT_hi[:, k, :], xT_lo[:, k, :], pair[bl], k == 0, k == KT - 1)
                    last.then_inc(unit_used, 1)
                    if j == 3 and not peeled:
                        pe.wait_ge(pair_free[1], i * 2 + b0)
                        turn_act()

            def down(i, u0, b0, n, per):
                for j in range(2 * per):
                    use(i * (2 * per) + (u0 + j))
                    bl = j // per
                    if j % per == 0:
                        pe.wait_ge(pair_free[bl], i * 2 + b0)
                    for kk in range(KU):
                        k = KU * (j % per) + kk
                        last = k_tile(j, kk, actT_hi[:, k, :], actT_lo[:, k, :], pair[bl], k == 0, k == KU * per - 1)
                    last.then_inc(unit_used, 1)

            for g in range(8):
                wait_read(pe, ("hA", g))
            for n, n0, ug, ud, bgt, bd in ((FF_A, 0, U_GUA, U_DA, B_GUA, B_DA), (FF_B, FF_A, U_GUB, U_DB, B_GUB, B_DB)):
                gate_up(0, ug, bgt, n0, True)
                with pe.Fori(1, n) as i:
                    gate_up(i, ug, bgt, n0, False)
                pe.wait_ge(pair_free[1], bd)
                turn_act()
                for q in range(2):
                    pe.wait_ge(ff_free[q], n0 + n)
                if n0 == 0:
                    with pe.Fori(0, 2) as i:
                        down(i, ud, bd, n, n * 4 // KU)
                else:
                    straight(ud, bd, 4, n * 4 // KU, lambda b, k: (actT_hi[:, k, :], actT_lo[:, k, :]))

            def normed(b, k):
                if b == 0 and k in (0, 12):
                    for g in (range(6) if k == 0 else (6, 7)):
                        wait_read(pe, ("hB", g))
                return xT_hi[:, k, :], xT_lo[:, k, :]

            straight(U_PG, B_PG, 4, UPB, normed)

        @block.scalar
        def _(act):
            f = nc.scalar.activation
            act.dma_start(rows[0:KT, :], A["attn_norm"][0].rearrange("(k p) -> k p", p=P)).then_inc(rows_landed, 16)
            act.dma_start(rows[KT:2 * KT, :], A["ffn_norm"][0].rearrange("(k p) -> k p", p=P)).then_inc(rows_landed, 16)
            act.dma_start(rows[2 * KT:3 * KT, :], A["ple_norm"][0].rearrange("(k p) -> k p", p=P)).then_inc(rows_landed, 16)
            for i, n in enumerate(("gdn_norm", "q_norm", "k_norm")):
                act.dma_start(rows[3 * KT + i:3 * KT + i + 1, :], A[n]).then_inc(rows_landed, 16)
            act.dma_start(p_in[:], A["p"][0, 0].rearrange("(t p) n -> p t n", p=P)).then_inc(p_landed, 16)
            act.dma_start(convw[:].rearrange("p (m j) -> p m j", j=CONV),
                          A["conv_w"][0].rearrange("(m p) j -> p m j", p=P)).then_inc(small_landed, 16)
            act.dma_start(a_log[:], A["A_log"].to_broadcast([P, HEADS])).then_inc(small_landed, 16)
            act.dma_start(dt_b[:], A["dt_bias"].to_broadcast([P, HEADS])).then_inc(small_landed, 16)
            act.dma_start(wba_raw[:], w_in[:, :, C_BA:C_MOBA]).then_inc(ba_landed, 16)

            def split(u, j):
                act.wait_ge(raw_landed[j % RING], (u - j % RING) * (16 // RING) + 16)
                if not isinstance(u, int) or u >= RING:
                    act.wait_ge(unit_used, u - (RING - 1))
                f(w_hi[j % RING][:], raw[j % RING][:], ACT.Copy).then_inc(hi_ready, 1)

            for t in range(NT):
                act.wait_ge(x_landed[t], 16)
                f(x_junk[:, :], h[:, t, :], ACT.Square, accum_out=x_ss[:, t:t + 1]).then_inc(x_sq, 1)
                if t == 0:
                    act.wait_ge(x_sq, 1)
            act.wait_ge(x_rstd, 2)
            for t in range(NT):
                f(h[:, t, :], h[:, t, :], ACT.Copy, scale=x_rs[:, t:t + 1]).then_inc(x_scaled, 1)
            split(0, 0)

            def post(step, b):
                bk, i, use_n = where((step, b))
                bh = heads(bk[:])
                c, hg = b % 2, b // 2
                ts = slice(c * P, c * P + P)
                B = G[c]
                hs = slice(HG * hg, HG * hg + HG)
                s = (step, b)
                if step == "gains":
                    wait_full(act, s)
                    f(gains[:, 0:NROW], bk[:, 0:NROW], ACT.Copy).then_inc(gain_s, 1)
                    read_out(s, f(gains[:, G_QS:G_QS + 1], bk[:, G_Q:G_Q + 1], ACT.Copy, scale=float(P) ** -0.5))
                    wait_read(act, s)
                    act.wait_ge(gain_s, 1)
                elif step in ("x", "hA", "hB"):
                    col = {"x": G_ATTN, "hA": G_FFN, "hB": G_PLE}[step]
                    wait_full(act, s)
                    for kk in range(2):
                        k = 2 * b + kk
                        f(xT_hi[:, k, :], bk[:, kk * TOK:(kk + 1) * TOK], ACT.Copy,
                          scale=gains[:, col + k:col + k + 1]).then_inc(x_hi, 1)
                elif step == "p":
                    wait_full(act, s)
                    f(pT_hi[:].rearrange("p k n -> p (k n)"), bk[:], ACT.Copy).then_inc(p_hi, 1)
                elif step == "ba":
                    wait_full(act, s)
                    f(sc["beta"][:], bk[:, 0:4 * HEADS].rearrange("p (t n) -> p t n", t=NT)[:, :, 0:HEADS],
                      ACT.Sigmoid).then_inc(beta_ready, 1)
                    act.wait_ge(small_landed, 48)
                    f(exp_a[:], a_log[:], ACT.Exp).then_inc(dt_act, 1)
                    act.wait_ge(dt_dve, 2)
                    f(sc["dt_exp"][:], sc["dt_abs"][:], ACT.Exp, scale=-1.0).then_inc(dt_act, 1)
                    act.wait_ge(dt_act, 2)
                    f(sc["dt_ln"][:], sc["dt_exp"][:], ACT.Ln, bias=1.0).then_inc(dt_act, 1)
                elif step == "gc":
                    wait_full(act, s)
                    f(sc["egc"][:], bk[:, 0:2 * HEADS].rearrange("p (t n) -> p t n", t=NT), ACT.Exp).then_inc(egc_ready, 1)
                elif step == "q_tok":
                    wait_full(act, s)
                    f(B["T"][:], bh, ACT.Square).then_inc(q_sq, 1)
                elif step == "k_tok":
                    wait_full(act, s)
                    f(B["TT"][:], bh, ACT.Square).then_inc(k_sq, 1)
                elif step == "qT":
                    wait_full(act, s)
                    read_out(s, f(ch[:, hs, ts], bh, ACT.Copy))
                elif step == "kT":
                    wait_full(act, s)
                    read_out(s, f(B["AT"][:], bh, ACT.Copy))
                elif step == "kbT":
                    wait_full(act, s)
                    read_out(s, f(ch[:, HEADS + HG * hg:HEADS + HG * hg + HG, ts], bh, ACT.Copy))
                elif step == "gcrow":
                    act.wait_ge(gap_ready, b + 1)
                    f(B["Y"][:], B["Y"][:], ACT.Exp).then_inc(exp_ready, 1)
                elif step == "T0":
                    wait_full(act, s)
                    act.wait_ge(kd_ready, b + 1)
                    read_out(s, f(B["T"][:], bh, ACT.Copy))
                elif step.startswith("TT"):
                    wait_full(act, s)
                    read_out(s, f(B["TT"][:], bh, ACT.Copy))
                elif step == "u":
                    wait_full(act, s)
                    read_out(s, f(B["T"][:], bh, ACT.Copy))
                elif step == "S":
                    wait_full(act, s)
                    read_out(s, f(state[:], bh, ACT.Copy))
                elif step == "o":
                    wait_read(act, s)
                    f(B["Y"][:], B["V"][:], ACT.Square).then_inc(o_sq, 1)
                elif step == "ogT":
                    wait_full(act, s)
                    f(og_hi[:, hs, ts], bh, ACT.Copy, scale=gains[:, G_GDN:G_GDN + 1]).then_inc(og_hi_ready, 1)
                elif step == "mT":
                    wait_full(act, s)
                    j = b // 2
                    col = G_QS if j < 2 else G_K
                    jh = j % 2
                    read_out(s, f(mT[j // 2][:, HG * jh:HG * jh + HG, ts], bh, ACT.Copy, scale=gains[:, col:col + 1]))
                elif step == "sc":
                    act.wait_ge(max_ready, 2 * (b + 1))
                    f(pr[c][:, 0:P], pr[c][:, 0:P], ACT.Exp, bias=nmax[c][:, 0:1],
                      accum_out=psum_p[c][:, 0:1]).then_inc(exp_done, 1)
                    f(pr[c][:, P:3 * P], pr[c][:, P:3 * P], ACT.Exp, bias=nmax[c][:, 1:2],
                      accum_out=psum_p[c][:, 1:2]).then_inc(exp_done, 1)
                elif step == "pT":
                    wait_full(act, s)
                    read_out(s, f(prT[b][:], bk[:, 0:3 * P], ACT.Copy))
                elif step == "pv":
                    wait_full(act, s)
                    f(om_hi[:, b, :], bk[:, 0:TOK], ACT.Copy).then_inc(om_hi_ready, 1)

            for s in FIRST:
                post(*s)
            for u in range(1, LEAD):
                split(u, u)

            def conv(i, bl):
                n = i * 2 + bl
                act.wait_ge(unit_used, n * UPB + UPB)
                for m in range(4):
                    t0 = i * HEADS + (4 * bl + m)
                    act.wait_ge(small_landed, 48)
                    cs = slice(m % 2 * TOK, (m % 2 + 1) * TOK)
                    f(mn[m // 2][:, cs], pair[bl][m // 2][:, cs], ACT.Copy, scale=convw[:, bass.ds(t0 * CONV + (CONV - 1), 1)]).then_inc(tap3, 1)
                for q in range(2):
                    act.wait_ge(taps, n * 12 + (10 + 2 * q))
                    f(sq[q][:], mn[q][:], ACT.Sigmoid).then_inc(conv_sig, 1)

            act.wait_ge(small_landed, 48)

            def qkv(i):
                for j in range(2 * UPB):
                    split(i * (2 * UPB) + (j + LEAD), j + LEAD)
                    if j % UPB == UPB - 1:
                        if j >= UPB:
                            act.wait_ge(pair_free[0], i * 2 + 2)
                        elif not isinstance(i, int):
                            act.wait_ge(pair_free[1], i * 2)
                        conv(i, j // UPB)

            qkv(0)
            with act.Fori(1, 3) as i:
                qkv(i)
            act.wait_ge(ba_landed, 16)
            f(wba_hi[:], wba_raw[:], ACT.Copy).then_inc(ba_hi, 1)
            for s in GATES:
                post(*s)

            def mix_end(b):
                wait_block(act, U_MIX + b * UPB + UPB - 1)
                n = B_MIX + b
                if b < 2:
                    if b == 0:
                        wait_pair_read(act, B_MIX - 1)
                    else:
                        wait_pair_read(act, n - 1)
                    for t in range(NT):
                        f(sq[t][:], pair[n % 2][t][:], ACT.Sigmoid).then_inc(z_sig, 1)
                elif b < 6:
                    if b == 2:
                        wait_pair_read(act, n - 1)
                    for t in range(NT):
                        if b > 2:
                            act.wait_ge(m_sum, 2 * (b - 3) + t + 1)
                        f(sq[t][:], pair[n % 2][t][:], ACT.Square).then_inc(m_sq, 1)
                else:
                    for t in range(NT):
                        f(mv[:, t, (b - 6) * CB:(b - 5) * CB], pair[n % 2][t][:], ACT.Copy).then_inc(pair_free[n % 2], 1)

            def res_end(last_unit, i, n):
                wait_block(act, last_unit)
                bno = (B_WO if i == 0 else B_DB) + n
                wait_pair_read(act, bno)
                for t in range(NT):
                    f(junk[:], h[:, t, n * CB:(n + 1) * CB], ACT.Square, accum_out=h_ss[i][:, t, n:n + 1]).then_inc(h_sq, 1)
                    act.wait_ge(h_sq, 8 * i + 2 * n + t + 1)

            for u in range(U_MIX, U_GUA):
                split(u + LEAD, u + LEAD)
                for k in range(2):
                    for s in AT[u][k]:
                        post(*s)
                if u < U_WO and (u + 1) % UPB == 0:
                    mix_end((u - U_MIX) // UPB)
                elif U_WO <= u < U_PP and (u + 1) % UPB == 0:
                    res_end(u, 0, (u - U_WO) // UPB)
                elif u >= U_PP:
                    wait_block(act, u)
                    n = u - U_PP
                    for t in range(NT):
                        f(pp[:, t, n * CB:(n + 1) * CB], pair[n % 2][t][:], ACT.Copy).then_inc(pair_free[n % 2], 1)

            act.wait_ge(h_rstd, 2)

            def turned(n, kt):
                for q in range(2):
                    act.wait_ge(ff_full[q], n + 1)
                    act.wait_ge(h_rstd, 2)
                    f(actT_hi[:, bass.ds(kt + 2 * q, 2), :], bg[q][:].rearrange("p (k n) -> p k n", k=2),
                      ACT.Copy).then_inc(act_hi_ready, 1)

            def gate_up(i, u0, b0, n0, peeled):
                for j in range(2 * UPB):
                    split(i * (2 * UPB) + (u0 + j + LEAD), j + LEAD)
                    if j == 3 and not peeled:
                        turned(i + (n0 - 1), i * 4 - 4)
                    if j == UPB - 1:
                        act.wait_ge(unit_used, i * (2 * UPB) + (u0 + UPB))
                        act.wait_ge(pair_free[1], i * 2 + b0)
                        for t in range(NT):
                            f(gate_s[t][:], pair[0][t][:], ACT.Sigmoid, scale=h_rs[0][:, t:t + 1]).then_inc(gate_sig, 1)

            for n, n0, ug, ud, bgt in ((FF_A, 0, U_GUA, U_DA, B_GUA), (FF_B, FF_A, U_GUB, U_DB, B_GUB)):
                gate_up(0, ug, bgt, n0, True)
                with act.Fori(1, n) as i:
                    gate_up(i, ug, bgt, n0, False)
                turned(n0 + n - 1, 4 * (n - 1))
                per = n * 4 // KU
                if n0 == 0:
                    with act.Fori(0, 2) as i:
                        for j in range(2 * per):
                            split(i * (2 * per) + (ud + j + LEAD), j + LEAD)
                else:
                    for j in range(4 * per):
                        split(ud + j + LEAD, j + LEAD)
                        for k in range(2):
                            for s in AT[ud + j][k]:
                                post(*s)
                        if (j + 1) % per == 0:
                            res_end(ud + j, 1, j // per)
            for u in range(U_PG, UNITS):
                if u + LEAD < UNITS:
                    split(u + LEAD, u + LEAD)
                for k in range(2):
                    for s in AT[u][k]:
                        post(*s)
                if u == U_PG + 4:
                    act.wait_ge(h_rstd, 4)
                if (u - U_PG + 1) % UPB == 0:
                    b = (u - U_PG) // UPB
                    wait_block(act, u)
                    if b:
                        act.wait_ge(out_ready, 2 * b)
                    for t in range(NT):
                        f(gate_s[t][:], pair[b % 2][t][:], ACT.Sigmoid, scale=h_rs[1][:, t:t + 1]).then_inc(pair_free[b % 2], 1)

        @block.vector
        def _(dve):
            v = nc.vector

            def split(u, j):
                dve.wait_ge(hi_ready, u + 1)
                v.tensor_tensor(w_lo[j % RING][:], raw[j % RING][:], w_hi[j % RING][:].bitcast(F32),
                                ALU.subtract).then_inc(lo_ready, 1)

            hi_base = {"x": 0, "hA": KT, "hB": 2 * KT}

            def post(step, b):
                bk, i, use_n = where((step, b))
                bh = heads(bk[:])
                c, hg = b % 2, b // 2
                ts = slice(c * P, c * P + P)
                B = G[c]
                hs = slice(HG * hg, HG * hg + HG)
                s = (step, b)
                if step in ("x", "hA", "hB"):
                    col = {"x": G_ATTN, "hA": G_FFN, "hB": G_PLE}[step]
                    dve.wait_ge(x_hi, hi_base[step] + 2 * b + 2)
                    for kk in range(2):
                        k = 2 * b + kk
                        m = v.scalar_tensor_tensor(out=xT_lo[:, k, :], in0=bk[:, kk * TOK:(kk + 1) * TOK],
                                                   scalar=gains[:, col + k:col + k + 1],
                                                   in1=xT_hi[:, k, :].bitcast(F32), op0=ALU.mult, op1=ALU.subtract)
                    read_out(s, m)
                elif step == "p":
                    dve.wait_ge(p_hi, 1)
                    read_out(s, v.tensor_tensor(pT_lo[:].rearrange("p k n -> p (k n)"), bk[:],
                                                pT_hi[:].rearrange("p k n -> p (k n)").bitcast(F32), ALU.subtract))
                elif step == "ba":
                    dve.wait_ge(beta_ready, 1)
                    dve.wait_ge(small_landed, 48)
                    read_out(s, v.tensor_tensor(
                        sc["dt_in"][:], bk[:, 0:4 * HEADS].rearrange("p (t n) -> p t n", t=NT)[:, :, HEADS:2 * HEADS],
                        dt_b[:].unsqueeze(1).to_broadcast([P, NT, HEADS]), ALU.add))
                    wait_read(dve, s)
                    v.tensor_scalar(sc["dt_sum"][:], sc["dt_in"][:], 0.0, None, ALU.max).then_inc(dt_dve, 1)
                    dve.wait_ge(dt_dve, 1)
                    v.scalar_tensor_tensor(out=sc["dt_abs"][:], in0=sc["dt_sum"][:], scalar=2.0, in1=sc["dt_in"][:],
                                           op0=ALU.mult, op1=ALU.subtract).then_inc(dt_dve, 1)
                    dve.wait_ge(dt_act, 3)
                    v.tensor_tensor(sc["dt_sum"][:], sc["dt_sum"][:], sc["dt_ln"][:], ALU.add).then_inc(dt_dve, 1)
                    dve.wait_ge(dt_dve, 3)
                    v.scalar_tensor_tensor(out=sc["g"][:], in0=sc["dt_sum"][:], scalar=-1.0,
                                           in1=exp_a[:].unsqueeze(1).to_broadcast([P, NT, HEADS]),
                                           op0=ALU.mult, op1=ALU.mult).then_inc(g_ready, 1)
                elif step == "gc":
                    dve.wait_ge(egc_ready, 1)
                    read_out(s, v.tensor_copy(sc["gc"][:], bk[:, 0:2 * HEADS].rearrange("p (t n) -> p t n", t=NT)))
                elif step == "q_tok":
                    dve.wait_ge(q_sq, b + 1)
                    v.reduce_sum(q_ss[c][:], B["T"][:], AX_X).then_inc(q_sum, 1)
                    dve.wait_ge(q_rstd, 2 * (b + 1))
                    read_out(s, v.tensor_tensor(B["Y"][:], bh, over_cols(q_rs[c][:]), ALU.mult))
                elif step == "k_tok":
                    dve.wait_ge(k_sq, b + 1)
                    v.reduce_sum(k_ss[c][:], B["TT"][:], AX_X).then_inc(k_sum, 1)
                    dve.wait_ge(k_rstd, 2 * (b + 1))
                    read_out(s, v.tensor_tensor(B["T"][:], bh, over_cols(k_rs[c][:]), ALU.mult))
                elif step == "v_tok":
                    wait_full(dve, s)
                    read_out(s, v.tensor_tensor(B["V"][:], bh, over_cols(sc["beta"][:, c, hs]), ALU.mult))
                elif step == "gcrow":
                    wait_full(dve, s)
                    wait_read(dve, ("gc", 0))
                    v.tensor_tensor(B["Y"][:], bh, over_cols(sc["gc"][:, c, hs]), ALU.subtract).then_inc(bank_free[i], 1)
                    wait_read(dve, s)
                    v.tensor_scalar(B["Y"][:], B["Y"][:], 0.0, None, ALU.min).then_inc(gap_ready, 1)
                elif step == "gramQ":
                    wait_full(dve, s)
                    dve.wait_ge(decay_ready, b + 1)
                    read_out(s, v.tensor_tensor(ch[:, 2 * HEADS + HG * hg:2 * HEADS + HG * hg + HG, ts], bh, B["Y"][:],
                                                ALU.mult))
                elif step == "gramA":
                    wait_full(dve, s)
                    read_out(s, v.tensor_tensor(B["AT"][:], bh, B["Y"][:], ALU.mult))
                    wait_read(dve, s)
                    v.tensor_tensor(B["Y"][:], B["AT"][:], over_heads(join0T[:]), ALU.mult).then_inc(tt_mid, 1)
                    dve.wait_ge(tt_mid, b + 1)
                    v.tensor_tensor(B["TT"][:], over_heads(ident[:]), B["Y"][:], ALU.subtract).then_inc(tt0, 1)
                elif step[0] == "Y":
                    wait_full(dve, s)
                    read_out(s, v.tensor_tensor(B["Y"][:], bh, over_heads(join[:, int(step[1:]), :]), ALU.mult))
                elif step == "ZT":
                    wait_full(dve, s)
                    read_out(s, v.tensor_tensor(B["TT"][:], B["TT"][:], bh, ALU.subtract))
                elif step[0] == "Z":
                    wait_full(dve, s)
                    read_out(s, v.tensor_tensor(B["T"][:], B["T"][:], bh, ALU.subtract))
                elif step == "ks":
                    wait_full(dve, s)
                    read_out(s, v.tensor_tensor(B["Y"][:], bh, over_cols(sc["egc"][:, c, hs]), ALU.mult))
                    wait_read(dve, s)
                    v.tensor_tensor(B["V"][:], B["V"][:], B["Y"][:], ALU.subtract).then_inc(r_ready, 1)
                elif step == "qs":
                    wait_full(dve, s)
                    dve.wait_ge(r_ready, (b + 1) // 2)
                    read_out(s, v.tensor_tensor(B["Y"][:], bh, over_cols(sc["egc"][:, c, hs]), ALU.mult))
                elif step == "o":
                    wait_full(dve, s)
                    if c:
                        wait_read(dve, ("qs", b))
                        read_out(s, v.tensor_tensor(B["V"][:], bh, B["Y"][:], ALU.add))
                    else:
                        read_out(s, v.tensor_copy(B["V"][:], bh))
                    dve.wait_ge(o_sq, b + 1)
                    v.reduce_sum(o_ss[c][:], B["Y"][:], AX_X).then_inc(o_sum, 1)
                    dve.wait_ge(o_rstd, 2 * (b + 1))
                    v.tensor_tensor(B["V"][:], B["V"][:], over_cols(o_rs[c][:]), ALU.mult).then_inc(o_scaled, 1)
                    dve.wait_ge(o_scaled, b + 1)
                    wait_pair_read(dve, B_MIX + 1)
                    wait_pair_read(dve, B_MIX)
                    v.tensor_tensor(B["V"][:], B["V"][:], heads(zg[:, c, hg * CB:(hg + 1) * CB]), ALU.mult).then_inc(og_ready, 1)
                elif step == "ogT":
                    dve.wait_ge(og_hi_ready, b + 1)
                    for j in range(HG):
                        hd = HG * hg + j
                        m = v.scalar_tensor_tensor(out=og_lo[:, hd, ts], in0=bh[:, j, :], scalar=gains[:, G_GDN:G_GDN + 1],
                                                   in1=og_hi[:, hd, ts].bitcast(F32), op0=ALU.mult, op1=ALU.subtract)
                    read_out(s, m)
                elif step == "sc":
                    wait_full(dve, s)
                    if b >= 2:
                        wait_full(dve, ("pT", b - 2))
                    read_out(s, v.tensor_tensor(pr[c][:], bk[:, 0:3 * P], causal[:], ALU.add))
                    wait_read(dve, s)
                    for q, (lo, up) in enumerate(((0, P), (P, 3 * P))):
                        v.tensor_reduce(nmax[c][:, q:q + 1], pr[c][:, lo:up], AX_X, ALU.max, negate=True).then_inc(max_ready, 1)
                    dve.wait_ge(exp_done, 2 * (b + 1))
                    v.reciprocal(rsum[c][:], psum_p[c][:]).then_inc(rsum_ready, 1)
                    dve.wait_ge(rsum_ready, b + 1)
                    v.tensor_scalar(pr[c][:, 0:P], pr[c][:, 0:P], rsum[c][:, 0:1], None, ALU.mult)
                    v.tensor_scalar(pr[c][:, P:3 * P], pr[c][:, P:3 * P], rsum[c][:, 1:2], None, ALU.mult).then_inc(p_ready, 1)
                elif step == "pv":
                    dve.wait_ge(om_hi_ready, b + 1)
                    read_out(s, v.tensor_tensor(om_lo[:, b, :], bk[:, 0:TOK], om_hi[:, b, :].bitcast(F32), ALU.subtract))

            for s in FIRST:
                post(*s)
            for u in range(LEAD):
                split(u, u)

            dve.wait_ge(small_landed, 48)

            def conv(i, bl):
                n = i * 2 + bl
                done = 0
                for tap in (2, 1, 0):
                    sh = CONV - 1 - tap
                    for m in range(4):
                        t0 = i * HEADS + (4 * bl + m)
                        if tap == 2:
                            dve.wait_ge(tap3, n * 4 + (m // 2 * 2 + 2))
                        else:
                            dve.wait_ge(taps, n * 12 + (done - 3))
                        o = mn[m // 2][:, m % 2 * TOK + sh:(m % 2 + 1) * TOK]
                        src = pair[bl][m // 2][:, m % 2 * TOK:(m % 2 + 1) * TOK - sh]
                        v.scalar_tensor_tensor(out=o, in0=src, scalar=convw[:, bass.ds(t0 * CONV + tap, 1)], in1=o,
                                               op0=ALU.mult, op1=ALU.add).then_inc(taps, 1)
                        done += 1
                for q in range(2):
                    dve.wait_ge(conv_sig, n * 2 + (q + 1))
                    t0 = i * HEADS + (4 * bl + 2 * q)
                    v.tensor_tensor(ch[:, bass.ds(t0, 2), :], mn[q][:].rearrange("p (m n) -> p m n", m=2),
                                    sq[q][:].rearrange("p (m n) -> p m n", m=2), ALU.mult).then_inc(pair_free[bl], 1)

            def qkv(i):
                for j in range(2 * UPB):
                    split(i * (2 * UPB) + (j + LEAD), j + LEAD)
                    if j % UPB == UPB - 1:
                        conv(i, j // UPB)

            qkv(0)
            with dve.Fori(1, 3) as i:
                qkv(i)
            dve.wait_ge(ba_hi, 1)
            v.tensor_tensor(wba_lo[:], wba_raw[:], wba_hi[:].bitcast(F32), ALU.subtract).then_inc(ba_lo, 1)
            for s in GATES:
                post(*s)

            def mix_end(b):
                n = B_MIX + b
                if b < 2:
                    for t in range(NT):
                        dve.wait_ge(z_sig, 2 * b + t + 1)
                        v.tensor_tensor(zg[:, t, b * CB:(b + 1) * CB], pair[n % 2][t][:], sq[t][:],
                                        ALU.mult).then_inc(pair_free[n % 2], 1)
                elif b < 6:
                    for t in range(NT):
                        i = 2 * (b - 2) + t
                        dve.wait_ge(m_sq, i + 1)
                        if b > 2:
                            wait_full(dve, ("mT", i - 2))
                        v.tensor_copy(mn[t][:], pair[n % 2][t][:]).then_inc(pair_free[n % 2], 1)
                        v.reduce_sum(m_ss[t][:], heads(sq[t][:]), AX_X).then_inc(m_sum, 1)
                    wait_pair_read(dve, n)
                    for t in range(NT):
                        i = 2 * (b - 2) + t
                        dve.wait_ge(m_rstd, 2 * (i + 1))
                        v.tensor_tensor(heads(mn[t][:]), heads(mn[t][:]), over_cols(m_rs[t][:]), ALU.mult).then_inc(mn_ready, 1)

            def res_end(last_unit, i, n):
                wait_block(dve, last_unit)
                bno = (B_WO if i == 0 else B_DB) + n
                if i == 0 and n == 0:
                    dve.wait_ge(x_again, 16)
                for t in range(NT):
                    o = h[:, t, n * CB:(n + 1) * CB]
                    v.tensor_tensor(o, o, pair[bno % 2][t][:], ALU.add).then_inc(pair_free[bno % 2], 1)
                if n == 3:
                    dve.wait_ge(h_sq, 8 * (i + 1))
                    v.reduce_sum(h_s[i][:], h_ss[i][:], AX_X).then_inc(h_sum, 1)

            for u in range(U_MIX, U_GUA):
                split(u + LEAD, u + LEAD)
                for k in range(2):
                    for s in AT[u][k]:
                        post(*s)
                if u < U_WO and (u + 1) % UPB == 0:
                    mix_end((u - U_MIX) // UPB)
                elif U_WO <= u < U_PP and (u + 1) % UPB == 0:
                    res_end(u, 0, (u - U_WO) // UPB)

            dve.wait_ge(h_rstd, 2)

            def turned(n, kt):
                for q in range(2):
                    dve.wait_ge(act_hi_ready, n * 2 + (q + 1))
                    ks = bass.ds(kt + 2 * q, 2)
                    v.tensor_tensor(actT_lo[:, ks, :], bg[q][:].rearrange("p (k n) -> p k n", k=2),
                                    actT_hi[:, ks, :].bitcast(F32), ALU.subtract).then_inc(ff_free[q], 1)

            def gate_up(i, u0, b0, n0, peeled):
                for j in range(2 * UPB):
                    split(i * (2 * UPB) + (u0 + j + LEAD), j + LEAD)
                    if j == 3 and not peeled:
                        turned(i + (n0 - 1), i * 4 - 4)
                    if j == UPB - 1:
                        for t in range(NT):
                            dve.wait_ge(gate_sig, i * 2 + (2 * n0 + t + 1))
                            v.scalar_tensor_tensor(out=gate_s[t][:], in0=pair[0][t][:], scalar=h_rs[0][:, t:t + 1],
                                                   in1=gate_s[t][:], op0=ALU.mult, op1=ALU.mult).then_inc(pair_free[0], 1)
                    if j == 2 * UPB - 1:
                        dve.wait_ge(unit_used, i * (2 * UPB) + (u0 + 2 * UPB))
                        dve.wait_ge(pair_free[0], i * 2 + (b0 + 2))
                        for t in range(NT):
                            v.scalar_tensor_tensor(out=act_s[t][:], in0=pair[1][t][:], scalar=h_rs[0][:, t:t + 1],
                                                   in1=gate_s[t][:], op0=ALU.mult, op1=ALU.mult).then_inc(pair_free[1], 1)

            for n, n0, ug, ud, bgt in ((FF_A, 0, U_GUA, U_DA, B_GUA), (FF_B, FF_A, U_GUB, U_DB, B_GUB)):
                gate_up(0, ug, bgt, n0, True)
                with dve.Fori(1, n) as i:
                    gate_up(i, ug, bgt, n0, False)
                turned(n0 + n - 1, 4 * (n - 1))
                per = n * 4 // KU
                if n0 == 0:
                    with dve.Fori(0, 2) as i:
                        for j in range(2 * per):
                            split(i * (2 * per) + (ud + j + LEAD), j + LEAD)
                            if (j + 1) % per == 0:
                                bl = j // per
                                dve.wait_ge(unit_used, i * (2 * per) + (ud + j + 1))
                                for t in range(NT):
                                    o = h[:, t, bass.ds(i * (2 * CB) + bl * CB, CB)]
                                    v.tensor_tensor(o, o, pair[bl][t][:], ALU.add).then_inc(pair_free[bl], 1)
                else:
                    for j in range(4 * per):
                        split(ud + j + LEAD, j + LEAD)
                        for k in range(2):
                            for s in AT[ud + j][k]:
                                post(*s)
                        if (j + 1) % per == 0:
                            res_end(ud + j, 1, j // per)
            for u in range(U_PG, UNITS):
                if u + LEAD < UNITS:
                    split(u + LEAD, u + LEAD)
                for k in range(2):
                    for s in AT[u][k]:
                        post(*s)
                if (u - U_PG + 1) % UPB == 0:
                    b = (u - U_PG) // UPB
                    cs = slice(b * CB, b * CB + CB)
                    wait_pair_read(dve, B_PG + b)
                    for t in range(NT):
                        v.tensor_tensor(gate_s[t][:], gate_s[t][:], pp[:, t, cs], ALU.mult).then_inc(pg_mul, 1)
                    for t in range(NT):
                        dve.wait_ge(pg_mul, 2 * b + t + 1)
                        v.tensor_tensor(h[:, t, cs], h[:, t, cs], gate_s[t][:], ALU.add).then_inc(out_ready, 1)


_INS = ["x", "p", "attn_norm", "w_in", "conv_w", "A_log", "dt_bias", "gdn_norm", "q_norm", "k_norm",
        "w_o", "ffn_norm", "w_gate", "w_up", "w_down", "ple_norm", "w_ple_gate", "w_ple_proj"]


def kernel(**inputs):
    import numpy as _np
    import concourse.bacc as _bacc
    from concourse import mybir as _mybir
    from concourse.bass_utils import run_bass_kernel_spmd as _run

    nc = _bacc.Bacc("TRN2", target_bir_lowering=False, num_devices=1)
    arrays, args = {}, {}
    for name in _INS:
        a = _np.ascontiguousarray(inputs[name])
        arrays[f"in_{name}_dram"] = a
        args[name] = nc.dram_tensor(f"in_{name}_dram", a.shape, _mybir.dt.from_np(a.dtype), kind="ExternalInput").ap()
    args["out"] = nc.dram_tensor("out_0_dram", (1, TOK, D), _mybir.dt.float32, kind="ExternalOutput").ap()
    build(nc, args)
    r = _run(nc, [arrays], core_ids=[0])
    return r.results[0]["out_0_dram"]
```

```python
from contextlib import ExitStack

import concourse.bass as bass
from concourse import mybir

ALU = mybir.AluOpType
ACT = mybir.ActivationFunctionType
AX_X = mybir.AxisListType.X
F32 = mybir.dt.float32
F32R = mybir.dt.float32r

P = 128
TOK = 256
NT = TOK // P
D = 2048
KT = D // P
CB = 512
FF = 5632
HEADS = 8
HG = 4
PLE = 256
CONV = 4
EPS = 1e-6
BANKS = 4
RING = 4
KU = 2
LEAD = 3
CHAN = 3 * HEADS
C_Z, C_BA, C_MOBA = 3 * HEADS * P, 4 * HEADS * P, 4 * HEADS * P + 2 * HEADS
LEVELS = 7
NEG = -1e30

UPB = KT // KU
U_QKV, B_QKV = 2 * UPB, 2
U_MIX, B_MIX = U_QKV + 6 * UPB, 8
U_WO, B_WO = U_MIX + 6 * UPB, 14
U_PP, B_PP = U_WO + 4 * UPB, 18
FF_A, FF_B = 6, 5
U_GUA, B_GUA = U_PP + 4, 22
U_DA, B_DA = U_GUA + FF_A * 2 * UPB, 22 + 2 * FF_A
U_GUB, B_GUB = U_DA + 4 * (FF_A * 4 // KU), B_DA + 4
U_DB, B_DB = U_GUB + FF_B * 2 * UPB, B_GUB + 2 * FF_B
U_PG, B_PG = U_DB + 4 * (FF_B * 4 // KU), B_DB + 4
UNITS = U_PG + 4 * UPB
assert not any(u % RING for u in (U_MIX, U_WO, U_PP, U_GUA, U_DA, U_GUB, U_DB, U_PG))

LATER = {"q_n": "q_tok", "k_n": "k_tok", "o_s": "o", "o_n": "o", "rest": "gcrow", "m_sq": "mT", "m_n": "mT"}


def chunk_steps(b):
    steps = ["q_tok", "k_tok", "q_n", "v_tok", "k_n", "qT", "kT", "kbT", "gcrow", "gramQ", "gramA", "T0"]
    for l in range(1, LEVELS - 1):
        steps += [f"Y{l}", f"Z{l}", f"TT{l}"]
    steps += [f"Y{LEVELS - 1}", "ZT"]
    if b % 2:
        steps += ["ks", "u", "qs", "o", "o_s", "rest", "o_n", "ogT"]
    else:
        steps += ["u", "S", "o", "o_s", "rest", "rest", "o_n", "ogT"]
    return [(s, b) for s in steps]


def plan():
    first = [("gains", 0)] + [("x", g) for g in range(KT // 2)] + [("p", 0)]
    gates = [("baT", 0), ("ba", 0), ("gc", 0)]
    delta = []
    even, odd = chunk_steps(0) + chunk_steps(2), chunk_steps(1) + chunk_steps(3)
    lag = 5
    for i in range(len(odd) + lag):
        delta += (odd[i - lag:i - lag + 1] if i >= lag else []) + even[i:i + 1]
    at = {u: [[], []] for u in range(UNITS)}
    slots = [(u, k) for u in range(U_MIX + LEAD, U_WO + 1) for k in range(2)]
    for n, s in enumerate(delta):
        u, k = slots[n * len(slots) // len(delta)]
        at[u][k].append(s)
    for j in range(4):
        for t in range(NT):
            u = U_MIX + (1 + j) * UPB + 2 + t
            at[u][1].append(("m_sq", 2 * j + t))
            at[u + 2][1].append(("m_n", 2 * j + t))
            at[u + 3 + t][1].append(("mT", 2 * j + t))
    for i, u in enumerate((U_WO - UPB, U_WO - UPB // 2, U_WO, U_WO + 2)):
        for k in range(2):
            at[u][k].append(("sc", 2 * i + k))
            at[u + 1][k].append(("pT", 2 * i + k))
            at[u + 2][k].append(("pv", 2 * i + k))
    for n in range(4):
        for g in range(2):
            at[(U_WO + (n + 1) * UPB if n < 3 else U_PP) + 2][g].append(("hA", 2 * n + g))
            at[(U_DB + (n + 1) * (FF_B * 4 // KU) if n < 3 else U_PG) + 3][g].append(("hB", 2 * n + g))
    order = first + gates + [s for u in range(UNITS) for k in at[u] for s in k]
    position = {s: n for n, s in enumerate(order)}
    reader = {"q_tok": "q_n", "k_tok": "k_n"}
    last_read, uses, banks = [-1] * BANKS, [0] * BANKS, {}
    for n, (s, b) in enumerate(order):
        if s not in LATER:
            i = last_read.index(min(last_read))
            assert last_read[i] < n
            banks[s, b] = i, uses[i]
            uses[i] += 1
            last_read[i] = position[reader.get(s, s), b]
    banks.update({(s, b): banks[LATER[s], b] for s, b in order if s in LATER})
    return first, at, banks


def build(nc, A):
    FIRST, AT, BANK_OF = plan()

    with ExitStack() as ctx:
        place = [16512]

        def sb(name, shape, dtype=F32, at=None):
            size = 4
            for n in shape[1:]:
                size *= n
            where = place[0] if at is None else at
            if at is None:
                place[0] += (size + 31) // 32 * 32
            return nc.alloc_sbuf_tensor_at(name, shape, dtype, offset=where)

        def sem(name):
            return ctx.enter_context(nc.semaphore(name))

        def bank(name):
            return ctx.enter_context(nc.psum_tensor(name, [P, CB], F32))

        xT_hi = sb("xT_hi", [P, KT, TOK], F32R)
        xT_lo = sb("xT_lo", [P, KT, TOK], F32R)
        raw = [sb(f"raw{i}", [P, KU, CB]) for i in range(RING)]
        w_hi = [sb(f"w_hi{i}", [P, KU, CB], F32R) for i in range(RING)]
        w_lo = [sb(f"w_lo{i}", [P, KU, CB], F32R) for i in range(RING)]
        mix = place[0]
        KIB = 1024
        place[0] += 64 * KIB
        ch = sb("ch", [P, CHAN, TOK], at=mix)
        og_hi = sb("og_hi", [P, HEADS, TOK], F32R, at=mix)
        og_lo = sb("og_lo", [P, HEADS, TOK], F32R, at=mix + 8 * KIB)
        om_hi = sb("om_hi", [P, HEADS, TOK], F32R, at=mix + 24 * KIB)
        om_lo = sb("om_lo", [P, HEADS, TOK], F32R, at=mix + 32 * KIB)
        names = ("AT", "T", "TT", "Y", "V", "KD")
        G = [{n: sb(f"{n}{c}", [P, HG, P], at=mix + (40 + 12 * c + 2 * i) * KIB) for i, n in enumerate(names)}
             for c in range(2)]
        actT_hi = sb("actT_hi", [P, 4 * FF_A, TOK], F32R, at=mix)
        actT_lo = sb("actT_lo", [P, 4 * FF_A, TOK], F32R, at=mix + 24 * KIB)
        gate_s = [sb(f"gate_s{t}", [P, CB], at=mix + (48 + 2 * t) * KIB) for t in range(NT)]
        act_s = [sb(f"act_s{t}", [P, CB], at=mix + (52 + 2 * t) * KIB) for t in range(NT)]
        junk = sb("junk", [P, CB], at=mix + 56 * KIB)
        x_junk = sb("x_junk", [P, D], at=mix)
        x_junk2 = sb("x_junk2", [P, D], at=mix + 8 * KIB)
        wba_raw = sb("wba_raw", [P, KT, 2 * HEADS], at=mix + 24 * KIB)
        wba_hi = sb("wba_hi", [P, KT, 2 * HEADS], F32R, at=mix + 25 * KIB)
        wba_lo = sb("wba_lo", [P, KT, 2 * HEADS], F32R, at=mix + 26 * KIB)
        baT = sb("baT", [2 * HEADS, TOK], at=mix + 27 * KIB)
        res = place[0]
        place[0] += 32 * KIB
        h = sb("h", [P, NT, D], at=res)
        mv = sb("mv", [P, NT, HEADS * P], at=res)
        zg = sb("zg", [P, NT, HEADS * P], at=res + 8 * KIB)
        mT = [sb("mqT", [P, HEADS, TOK], at=res + 16 * KIB), sb("mkT", [P, HEADS, TOK], at=res + 24 * KIB)]
        pp = sb("pp", [P, NT, D], at=res + 16 * KIB)
        sq = [sb(f"sq{t}", [P, CB]) for t in range(NT)]
        mn = [sb(f"mn{t}", [P, CB]) for t in range(NT)]
        state = sb("state", [P, HG, P])
        pr = [sb(f"pr{i}", [P, 3 * P]) for i in range(2)]
        prT = [s[:, 0:3 * P] for s in sq]
        p_in = sb("p_in", [P, NT, PLE])
        pT_hi = sb("pT_hi", [P, PLE // P, TOK], F32R)
        pT_lo = sb("pT_lo", [P, PLE // P, TOK], F32R)
        ident = sb("ident", [P, P])
        triu = sb("triu", [P, P])
        ones = sb("ones", [P, P])
        join = sb("join", [P, LEVELS, P])
        join0T = sb("join0T", [P, P])
        causal = sb("causal", [P, 3 * P])
        NROW = 3 * KT + 3
        rows = sb("rows", [NROW, P])
        gains = sb("gains", [P, NROW + 1])
        G_ATTN, G_FFN, G_PLE, G_GDN, G_Q, G_K, G_QS = 0, KT, 2 * KT, 3 * KT, 3 * KT + 1, 3 * KT + 2, 3 * KT + 3
        convw = sb("convw", [P, CHAN * CONV])
        a_log = sb("a_log", [P, HEADS])
        dt_b = sb("dt_b", [P, HEADS])
        exp_a = sb("exp_a", [P, HEADS])
        sc = {n: sb(n, [P, NT, HEADS]) for n in ("beta", "dt_in", "dt_abs", "dt_exp", "dt_ln", "dt_sum", "g", "gc", "egc")}
        warm = sb("warm", [P, 1])
        half = sb("half", [P, 2 * HEADS])
        x_ss, x_ms, x_rs = (sb(n, [P, NT]) for n in ("x_ss", "x_ms", "x_rs"))
        q_ss, q_ms, q_rs, k_ss, k_ms, k_rs, o_ss, o_ms, o_rs = (
            [sb(f"{n}{c}", [P, HG]) for c in range(2)]
            for n in ("q_ss", "q_ms", "q_rs", "k_ss", "k_ms", "k_rs", "o_ss", "o_ms", "o_rs"))
        m_ss, m_ms, m_rs = ([sb(f"{n}{t}", [P, HG]) for t in range(NT)] for n in ("m_ss", "m_ms", "m_rs"))
        nmax, psum_p, rsum = ([sb(f"{n}{i}", [P, 2]) for i in range(2)] for n in ("nmax", "psum_p", "rsum"))
        h_ss = [sb(f"h_ss{i}", [P, NT, 4]) for i in range(2)]
        h_s, h_ms, h_rs = ([sb(f"{n}{i}", [P, NT]) for i in range(2)] for n in ("h_s", "h_ms", "h_rs"))

        pair = [[bank(f"pair{i}{t}") for t in range(2)] for i in range(2)]
        bg = [bank(f"bg{i}") for i in range(BANKS)]

        raw_landed = [sem(f"raw_landed{i}") for i in range(RING)]
        hi_ready, lo_ready, unit_used = sem("hi_ready"), sem("lo_ready"), sem("unit_used")
        pair_free = [sem("pair_free0"), sem("pair_free1")]
        bank_full = [sem(f"bank_full{i}") for i in range(BANKS)]
        bank_free = [sem(f"bank_free{i}") for i in range(BANKS)]
        x_landed, p_landed = [sem("x_landed0"), sem("x_landed1")], sem("p_landed")
        x_again = [sem(f"x_again{n}") for n in range(4)]
        small_landed, rows_landed, ba_landed = sem("small_landed"), sem("rows_landed"), sem("ba_landed")
        masks_ready, consts_ready, out_landed = sem("masks_ready"), sem("consts_ready"), sem("out_landed")
        x_sq, x_rstd, x_scaled = [sem("x_sq0"), sem("x_sq1")], sem("x_rstd"), sem("x_scaled")
        gain_s, x_hi, p_hi, ba_hi, ba_lo = sem("gain_s"), sem("x_hi"), sem("p_hi"), sem("ba_hi"), sem("ba_lo")
        tap3, taps, conv_sig = sem("tap3"), sem("taps"), sem("conv_sig")
        beta_ready, dt_dve, dt_act, g_ready, egc_ready = (
            sem(n) for n in ("beta_ready", "dt_dve", "dt_act", "g_ready", "egc_ready"))
        q_sq, q_sum, q_rstd, k_sq, k_sum, k_rstd, kb_ready = (
            sem(n) for n in ("q_sq", "q_sum", "q_rstd", "k_sq", "k_sum", "k_rstd", "kb_ready"))
        gtri_ready, gap_ready, exp_ready, decay_ready, kd_ready, tt_mid = (
            sem(n) for n in ("gtri_ready", "gap_ready", "exp_ready", "decay_ready", "kd_ready", "tt_mid"))
        tt0, r_ready, o_sq, o_sum, o_rstd, o_scaled, og_ready, og_hi_ready = (
            sem(n) for n in ("tt0", "r_ready", "o_sq", "o_sum", "o_rstd", "o_scaled", "og_ready", "og_hi_ready"))
        z_sig, m_sq, m_sum, m_rstd, mn_ready = (sem(n) for n in ("z_sig", "m_sq", "m_sum", "m_rstd", "mn_ready"))
        max_ready, exp_done, rsum_ready, p_ready, om_hi_ready = (
            sem(n) for n in ("max_ready", "exp_done", "rsum_ready", "p_ready", "om_hi_ready"))
        h_sq, h_sum, h_rstd, h_hi = sem("h_sq"), sem("h_sum"), sem("h_rstd"), sem("h_hi")
        gate_sig, act_hi_ready = sem("gate_sig"), sem("act_hi_ready")
        ff_full, ff_free = [sem("ff_full0"), sem("ff_full1")], [sem("ff_free0"), sem("ff_free1")]
        pg_mul, out_ready = sem("pg_mul"), sem("out_ready")

        def where(step):
            i, use = BANK_OF[step]
            return bg[i], i, use

        def wait_full(eng, step):
            _, i, use = where(step)
            eng.wait_ge(bank_full[i], use + 1)

        def wait_read(eng, step):
            _, i, use = where(step)
            eng.wait_ge(bank_free[i], use + 1)

        def read_out(step, instruction):
            instruction.then_inc(bank_free[where(step)[1]], 1)

        def heads(ap):
            return ap.rearrange("p (h n) -> p h n", h=HG)

        def over_cols(ap):
            return ap.unsqueeze(2).to_broadcast([P, HG, P])

        def over_heads(ap):
            return ap.unsqueeze(1).to_broadcast([P, HG, P])

        def wait_block(eng, last_unit):
            eng.wait_ge(unit_used, last_unit + 1)

        def wait_pair_read(eng, block):
            eng.wait_ge(pair_free[block % 2], 2 * (block // 2 + 1))

        w_in = A["w_in"][0].rearrange("(k p) n -> p k n", p=P)
        w_o = A["w_o"][0].rearrange("(k p) n -> p k n", p=P)
        w_gate = A["w_gate"][0].rearrange("(k p) n -> p k n", p=P)
        w_up = A["w_up"][0].rearrange("(k p) n -> p k n", p=P)
        w_down = A["w_down"][0].rearrange("(k p) n -> p k n", p=P)
        w_pg = A["w_ple_gate"][0].rearrange("(k p) n -> p k n", p=P)
        w_pp = A["w_ple_proj"][0].rearrange("(k p) n -> p k n", p=P)
        x_d = A["x"][0].rearrange("(t p) n -> p t n", p=P)
        out_d = A["out"][0].rearrange("(t p) n -> p t n", p=P)

        block = ctx.enter_context(nc.Block())

        @block.sync
        def _(sp):
            def load(u, j, w, k, col):
                if not isinstance(u, int) or u >= RING:
                    sp.wait_ge(lo_ready, u - (RING - 1))
                sp.dma_start(raw[j % RING][:], w[:, k:k + KU, bass.ds(col, CB)]).then_inc(raw_landed[j % RING], 16)

            for t in range(NT):
                for half_cols in (slice(0, D // 2), slice(D // 2, D)):
                    sp.dma_start(h[:, t, half_cols], x_d[:, t, half_cols]).then_inc(x_landed[t], 16)
            for j in range(2 * UPB):
                load(j, j, w_in, KU * (j % UPB), C_Z + j // UPB * CB)
                if j == RING - 1:
                    sp.dma_start(p_in[:], A["p"][0, 0].rearrange("(t p) n -> p t n", p=P)).then_inc(p_landed, 16)
                    sp.dma_start(convw[:].rearrange("p (m j) -> p m j", j=CONV),
                                  A["conv_w"][0].rearrange("(m p) j -> p m j", p=P)).then_inc(small_landed, 16)
                    sp.dma_start(a_log[:], A["A_log"].to_broadcast([P, HEADS])).then_inc(small_landed, 16)
                    sp.dma_start(dt_b[:], A["dt_bias"].to_broadcast([P, HEADS])).then_inc(small_landed, 16)
                    sp.dma_start(wba_raw[:], w_in[:, :, C_BA:C_MOBA]).then_inc(ba_landed, 16)
            with sp.Fori(0, 3) as i:
                for j in range(2 * UPB):
                    load(i * (2 * UPB) + (U_QKV + j), j, w_in, KU * (j % UPB), i * (2 * CB) + j // UPB * CB)
            with sp.Fori(0, 3) as i:
                for j in range(2 * UPB):
                    load(i * (2 * UPB) + (U_MIX + j), j, w_in, KU * (j % UPB), i * (2 * CB) + (C_MOBA + j // UPB * CB))
            for b in range(4):
                for j in range(UPB):
                    if b == 1 and j % 2 == 0:
                        if j == 0:
                            for s in (("pv", HEADS - 2), ("pv", HEADS - 1), ("ogT", 2), ("ogT", 3)):
                                wait_read(sp, s)
                        n = j // 2
                        sp.dma_start(h[:, :, n * CB:(n + 1) * CB], x_d[:, :, n * CB:(n + 1) * CB]).then_inc(x_again[n], 16)
                    load(U_WO + b * UPB + j, j, w_o, KU * j, b * CB)
            for b in range(4):
                load(U_PP + b, b, w_pp, 0, b * CB)
            for u0, u1, n, at in ((U_GUA, U_DA, FF_A, 0), (U_GUB, U_DB, FF_B, FF_A)):
                with sp.Fori(0, n) as i:
                    for j in range(2 * UPB):
                        w = w_gate if j < UPB else w_up
                        load(i * (2 * UPB) + (u0 + j), j, w, KU * (j % UPB), i * CB + at * CB)
                per = n * 4 // KU
                with sp.Fori(0, 2) as i:
                    for j in range(2 * per):
                        load(i * (2 * per) + (u1 + j), j, w_down, at * 4 + KU * (j % per),
                             i * (2 * CB) + j // per * CB)
            with sp.Fori(0, 2) as i:
                for j in range(2 * UPB):
                    load(i * (2 * UPB) + (U_PG + j), j, w_pg, KU * (j % UPB), i * (2 * CB) + j // UPB * CB)
            for b in range(3):
                sp.wait_ge(out_ready, NT * (b + 1))
                sp.dma_start(out_d[:, :, b * CB:(b + 1) * CB], h[:, :, b * CB:(b + 1) * CB]).then_inc(out_landed, 16)
            for t in range(NT):
                sp.wait_ge(out_ready, NT * 3 + t + 1)
                sp.dma_start(out_d[:, t, 3 * CB:], h[:, t, 3 * CB:]).then_inc(out_landed, 16)
            sp.wait_ge(out_landed, 16 * (3 + NT))

        @block.gpsimd
        def _(pool):
            g = nc.gpsimd
            n = 0

            def mask(ins):
                nonlocal n
                n += 1
                ins.then_inc(masks_ready, 1)
                pool.wait_ge(masks_ready, n)

            mask(g.memset(half[:], -0.5))
            mask(g.memset(ones[:], 1.0))
            mask(g.memset(ident[:], 0.0))
            g.affine_select(out=ident[:], in_=ident[:], compare_op=ALU.not_equal, fill=1.0, base=0,
                            pattern=[[-1, P]], channel_multiplier=1).then_inc(consts_ready, 1)

            def rstd(out, mid, ss, scale, eps, done, count):
                g.tensor_scalar(mid, ss, scale, eps, ALU.mult, ALU.add).then_inc(done, 1)
                pool.wait_ge(done, 2 * count + 1)
                g.tensor_tensor(out, mid, half[:, 0:mid.shape[1]], ALU.pow).then_inc(done, 1)

            for t in range(NT):
                pool.wait_ge(x_sq[t], 1)
                rstd(x_rs[:, t:t + 1], x_ms[:, t:t + 1], x_ss[:, t:t + 1], 1.0 / D, EPS, x_rstd, t)

            mask(g.affine_select(out=triu[:], in_=ones[:], compare_op=ALU.is_ge, fill=0.0, base=0,
                                 pattern=[[1, P]], channel_multiplier=-1))
            mask(g.memset(causal[:], 0.0))
            for o in (0, 2 * P):
                mask(g.affine_select(out=causal[:, o:o + P], in_=causal[:, o:o + P], compare_op=ALU.is_ge, fill=NEG,
                                     base=0, pattern=[[-1, P]], channel_multiplier=1))
            mask(g.memset(join[:], 0.0))
            for l in range(LEVELS):
                b = 1 << l
                m = join[:, l, :].rearrange("p (j two b) -> p j two b", two=2, b=b)[:, :, 0, :]
                o = ones[:].rearrange("p (j two b) -> p j two b", two=2, b=b)[:, :, 0, :]
                mask(g.affine_select(out=m, in_=o, compare_op=ALU.is_ge, fill=0.0, base=-b,
                                     pattern=[[-2 * b, P // (2 * b)], [0, b]], channel_multiplier=1))
                mask(g.affine_select(out=m, in_=m, compare_op=ALU.is_ge, fill=0.0, base=2 * b - 1,
                                     pattern=[[2 * b, P // (2 * b)], [0, b]], channel_multiplier=-1))
            mask(g.memset(join0T[:], 0.0))
            m = join0T[:].rearrange("p (j two) -> p j two", two=2)[:, :, 1]
            mask(g.affine_select(out=m, in_=m, compare_op=ALU.not_equal, fill=1.0, base=0,
                                 pattern=[[-2, P // 2]], channel_multiplier=1))
            g.memset(join0T[:, 0:1], 0.0).then_inc(consts_ready, 1)

            def post(step, b):
                c, hg = b % 2, b // 2
                B = G[c]
                hs = slice(HG * hg, HG * hg + HG)
                if step == "q_tok":
                    pool.wait_ge(q_sum, b + 1)
                    rstd(q_rs[c][:], q_ms[c][:], q_ss[c][:], float(P), P * EPS, q_rstd, b)
                elif step == "k_tok":
                    pool.wait_ge(k_sum, b + 1)
                    rstd(k_rs[c][:], k_ms[c][:], k_ss[c][:], 1.0, EPS, k_rstd, b)
                elif step == "k_n":
                    wait_read(pool, (step, b))
                    g.tensor_tensor(B["TT"][:], B["T"][:], over_cols(sc["beta"][:, c, hs]),
                                    ALU.mult).then_inc(kb_ready, 1)
                elif step == "kbT":
                    wait_full(pool, (step, b))
                    g.tensor_tensor(B["TT"][:], over_heads(triu[:]), over_cols(sc["g"][:, c, hs]),
                                    ALU.mult).then_inc(gtri_ready, 1)
                elif step == "gcrow":
                    pool.wait_ge(exp_ready, b + 1)
                    g.tensor_tensor(B["KD"][:], B["T"][:], B["Y"][:, :, P - 1:P].to_broadcast([P, HG, P]),
                                    ALU.mult).then_inc(kd_ready, 1)
                    pool.wait_ge(kd_ready, b + 1)
                    g.tensor_tensor(B["Y"][:], B["Y"][:], over_heads(triu[:]), ALU.mult).then_inc(decay_ready, 1)
                elif step == "m_sq":
                    pool.wait_ge(m_sum, b + 1)
                    rstd(m_rs[c][:], m_ms[c][:], m_ss[c][:], 1.0 / P, EPS, m_rstd, b)
                elif step == "o_s":
                    pool.wait_ge(o_sum, b + 1)
                    rstd(o_rs[c][:], o_ms[c][:], o_ss[c][:], 1.0 / P, EPS, o_rstd, b)

            pool.wait_ge(g_ready, 1)
            for u in range(U_MIX, U_WO + 1):
                for k in range(2):
                    for s in AT[u][k]:
                        post(*s)
            for i in range(2):
                pool.wait_ge(h_sum, i + 1)
                rstd(h_rs[i][:], h_ms[i][:], h_s[i][:], 1.0 / D, EPS, h_rstd, i)

        @block.tensor
        def _(pe):
            mm, tp = nc.tensor.matmul, nc.tensor.transpose

            def use(u):
                pe.wait_ge(lo_ready, u + 1)

            def k_tile(j, kk, hi, lo, banks, first, last):
                wh, wl = w_hi[j % RING][:, kk, :], w_lo[j % RING][:, kk, :]
                for t in range(NT):
                    ts = slice(t * P, t * P + P)
                    mm(banks[t][:], hi[:, ts], wh, start=first, stop=False)
                    mm(banks[t][:], hi[:, ts], wl, start=False, stop=False)
                    m = mm(banks[t][:], lo[:, ts], wh, start=False, stop=last)
                return m

            def k_tile_ba(k, bk):
                o = bk[0:2 * HEADS, 0:TOK]
                mm(o, wba_hi[:, k, :], xT_hi[:, k, :], start=(k == 0), stop=False)
                mm(o, wba_lo[:, k, :], xT_hi[:, k, :], start=False, stop=False)
                return mm(o, wba_hi[:, k, :], xT_lo[:, k, :], start=False, stop=(k == KT - 1))

            def burst(s):
                step, b = s
                if step in LATER:
                    return
                bk, i, use_n = where(s)
                c, hg = b % 2, b // 2
                if use_n:
                    pe.wait_ge(bank_free[i], use_n)
                bh = heads(bk[:])
                last = None
                if step == "gains":
                    pe.wait_ge(rows_landed, 16 * 6)
                    pe.wait_ge(consts_ready, 1)
                    last = tp(bk[:, 0:NROW], rows[:], ident[0:NROW, 0:NROW])
                elif step in ("x", "hA", "hB"):
                    if step == "x":
                        if b == 0:
                            pe.wait_ge(x_scaled, NT)
                    elif b % 2 == 0:
                        block = (B_WO if step == "hA" else B_DB) + b // 2
                        wait_pair_read(pe, block)
                    for kk in range(2):
                        for t in range(NT):
                            k = 2 * b + kk
                            last = tp(bk[:, kk * TOK + t * P:kk * TOK + t * P + P], h[:, t, k * P:(k + 1) * P], ident[:])
                elif step == "p":
                    pe.wait_ge(p_landed, 16)
                    for kk in range(2):
                        for t in range(NT):
                            last = tp(bk[:, kk * TOK + t * P:kk * TOK + t * P + P], p_in[:, t, kk * P:(kk + 1) * P], ident[:])
                elif step == "ba":
                    wait_read(pe, ("baT", 0))
                    for t in range(NT):
                        last = tp(bk[:, t * 2 * HEADS:(t + 1) * 2 * HEADS], baT[:, t * P:(t + 1) * P],
                                  ident[0:2 * HEADS, 0:2 * HEADS])
                elif step == "gc":
                    pe.wait_ge(g_ready, 1)
                    pe.wait_ge(consts_ready, 2)
                    for t in range(NT):
                        last = mm(bk[:, t * HEADS:(t + 1) * HEADS], triu[:], sc["g"][:, t, :], start=True, stop=True)
                elif step == "mT":
                    pe.wait_ge(mn_ready, b + 1)
                    for j in range(HG):
                        last = tp(bh[:, j, :], mn[c][:, j * P:(j + 1) * P], ident[:])
                elif step == "sc":
                    for j in (b // HG, 2 + b // HG):
                        for t in range(NT):
                            wait_read(pe, ("mT", 2 * j + t))
                    mm(bk[:, 0:P], mT[0][:, b, 0:P], mT[1][:, b, 0:P], start=True, stop=True)
                    last = mm(bk[:, P:3 * P], mT[0][:, b, P:TOK], mT[1][:, b, :], start=True, stop=True)
                elif step == "pT":
                    pe.wait_ge(p_ready, b + 1)
                    for j in range(3):
                        last = tp(bk[:, j * P:(j + 1) * P], pr[c][:, j * P:(j + 1) * P], ident[:])
                elif step == "pv":
                    wait_read(pe, ("pT", b))
                    wait_pair_read(pe, B_MIX + 4 + b // HG)
                    cs = slice(b * P, b * P + P)
                    mm(bk[:, 0:TOK], mv[:, 0, cs], prT[c][:, 0:TOK], start=True, stop=False, skip_group_check=True)
                    last = mm(bk[:, P:TOK], mv[:, 1, cs], prT[c][:, TOK:3 * P], start=False, stop=True,
                              skip_group_check=True)
                else:
                    last = delta(step, b, bh, G[c], c, hg)
                last.then_inc(bank_full[i], 1)

            def delta(step, b, bh, B, c, hg):
                ts = slice(c * P, c * P + P)
                last = None
                prev = {s: p for p, s in zip([x[0] for x in chunk_steps(b)], [x[0] for x in chunk_steps(b)][1:])}.get(step)
                if step == "q_tok":
                    if b < 2:
                        for q in range(2):
                            wait_pair_read(pe, B_MIX - 2 + q)
                    else:
                        wait_read(pe, ("ogT", b - 2))
                elif step == "k_tok" or step == "v_tok":
                    pass
                elif step == "qT":
                    wait_read(pe, ("q_tok", b))
                elif step == "kT":
                    wait_read(pe, ("k_tok", b))
                elif step == "kbT":
                    pe.wait_ge(kb_ready, b + 1)
                elif step == "gcrow":
                    pe.wait_ge(gtri_ready, b + 1)
                elif step == "gramQ":
                    for s in ("qT", "kT", "kbT"):
                        wait_read(pe, (s, b))
                elif step == "gramA":
                    pass
                elif step == "T0":
                    pe.wait_ge(tt0, b + 1)
                elif step == "ks":
                    wait_read(pe, (prev, b))
                    wait_read(pe, ("S", b - 1))
                elif step == "u" and c:
                    pe.wait_ge(r_ready, (b + 1) // 2)
                elif step == "qs":
                    pass
                elif step == "S":
                    wait_read(pe, ("u", b))
                    pe.wait_ge(kd_ready, b + 1)
                elif step == "o":
                    wait_read(pe, ("u", b))
                    wait_read(pe, ("gramQ", b))
                elif step == "ogT":
                    pe.wait_ge(og_ready, b + 1)
                else:
                    wait_read(pe, (prev, b))
                for j in range(HG):
                    hd = HG * hg + j
                    o = bh[:, j, :]
                    if step in ("q_tok", "k_tok", "v_tok"):
                        base = {"q_tok": 0, "k_tok": HEADS, "v_tok": 2 * HEADS}[step]
                        last = tp(o, ch[:, base + hd, ts], ident[:])
                    elif step in ("qT", "kT", "kbT", "T0", "ogT") or step.startswith("TT"):
                        src = {"qT": "Y", "kT": "T", "kbT": "TT", "T0": "TT", "ogT": "V"}.get(step, "T")
                        last = tp(o, B[src][:, j, :], ident[:])
                    elif step == "gcrow":
                        last = mm(o, ones[:], B["TT"][:, j, :], start=True, stop=True)
                    else:
                        l, r = {
                            "gramQ": lambda: (B["AT"][:, j, :], ch[:, hd, ts]),
                            "gramA": lambda: (B["AT"][:, j, :], ch[:, HEADS + hd, ts]),
                            "Y": lambda: (B["AT"][:, j, :], B["T"][:, j, :]),
                            "Z": lambda: (B["TT"][:, j, :], B["Y"][:, j, :]),
                            "ZT": lambda: (B["Y"][:, j, :], B["TT"][:, j, :]),
                            "ks": lambda: (ch[:, HEADS + hd, ts], state[:, j, :]),
                            "qs": lambda: (ch[:, hd, ts], state[:, j, :]),
                            "u": lambda: (B["TT"][:, j, :], B["V"][:, j, :]),
                            "S": lambda: (B["KD"][:, j, :], B["T"][:, j, :]),
                            "o": lambda: (ch[:, 2 * HEADS + hd, ts], B["T"][:, j, :]),
                        }[step if step in ("gramQ", "gramA", "ZT", "ks", "qs", "u", "S", "o") else step[0]]()
                        last = mm(o, l, r, start=True, stop=True)
                return last

            for s in FIRST:
                burst(s)
            for b in range(2):
                if b == 1:
                    pe.wait_ge(ba_lo, 1)
                    bk, i, use_n = where(("baT", 0))
                    pe.wait_ge(bank_free[i], use_n)
                for j in range(UPB):
                    use(b * UPB + j)
                    for kk in range(KU):
                        k = KU * j + kk
                        if b == 0 and kk == 0:
                            wait_read(pe, ("x", j))
                        last = k_tile(j, kk, xT_hi[:, k, :], xT_lo[:, k, :], pair[b], k == 0, k == KT - 1)
                        if b == 1:
                            ba = k_tile_ba(k, bk)
                    last.then_inc(unit_used, 1)

            ba.then_inc(bank_full[i], 1)

            def qkv(i, first):
                for j in range(2 * UPB):
                    use(i * (2 * UPB) + (U_QKV + j))
                    bl = j // UPB
                    if j % UPB == 0:
                        pe.wait_ge(pair_free[bl], i * 2 + B_QKV)
                    for kk in range(KU):
                        k = KU * (j % UPB) + kk
                        for m in range(4):
                            o = pair[bl][m // 2][:, m % 2 * TOK:(m % 2 + 1) * TOK]
                            ms = slice(m * P, m * P + P)
                            wh, wl = w_hi[j % RING][:, kk, ms], w_lo[j % RING][:, kk, ms]
                            mm(o, wh, xT_hi[:, k, :], start=(k == 0 and m % 2 == 0), stop=False, skip_group_check=True)
                            mm(o, wh, xT_lo[:, k, :], start=False, stop=False, skip_group_check=True)
                            last = mm(o, wl, xT_hi[:, k, :], start=False, stop=(k == KT - 1 and m % 2 == 1),
                                      skip_group_check=True)
                    last.then_inc(unit_used, 1)
                    if first and j in (1, 5):
                        burst(("ba" if j == 1 else "gc", 0))

            qkv(0, True)
            with pe.Fori(1, 3) as i:
                qkv(i, False)

            def straight(u0, b0, blocks, per, hi_lo, behind_3=None):
                for b in range(blocks):
                    pe.wait_ge(pair_free[(b0 + b) % 2], 2 * ((b0 + b) // 2))
                    for j in range(per):
                        u = u0 + b * per + j
                        use(u)
                        for kk in range(KU):
                            k = KU * j + kk
                            hi, lo = hi_lo(b, k)
                            last = k_tile(u, kk, hi, lo, pair[(b0 + b) % 2], k == 0, k == KU * per - 1)
                            if kk == KU - 1:
                                last.then_inc(unit_used, 1)
                            for s in AT[u][kk]:
                                burst(s)
                        if behind_3 and b == 0 and j == 3:
                            behind_3()

            straight(U_MIX, B_MIX, 6, UPB, lambda b, k: (xT_hi[:, k, :], xT_lo[:, k, :]))

            def mixed(b, k):
                if b == 0 and k in (0, HG):
                    for c in range(2):
                        wait_read(pe, ("ogT", k // HG * 2 + c))
                if b == 0 and k >= HEADS:
                    wait_read(pe, ("pv", k - HEADS))
                if k < HEADS:
                    return og_hi[:, k, :], og_lo[:, k, :]
                return om_hi[:, k - HEADS, :], om_lo[:, k - HEADS, :]

            straight(U_WO, B_WO, 4, UPB, mixed)
            straight(U_PP, B_PP, 4, 1, lambda b, k: (pT_hi[:, k, :], pT_lo[:, k, :]))

            def turn_act():
                for q in range(2):
                    for kk in range(2):
                        for t in range(NT):
                            cs = slice((2 * q + kk) * P, (2 * q + kk + 1) * P)
                            m = tp(bg[q][:, kk * TOK + t * P:kk * TOK + t * P + P], act_s[t][:, cs], ident[:])
                    m.then_inc(ff_full[q], 1)

            def gate_up(i, u0, b0, n0, peeled):
                for j in range(2 * UPB):
                    use(i * (2 * UPB) + (u0 + j))
                    bl = j // UPB
                    if j % UPB == 0:
                        pe.wait_ge(pair_free[bl], i * 2 + b0)
                    for kk in range(KU):
                        k = KU * (j % UPB) + kk
                        last = k_tile(j, kk, xT_hi[:, k, :], xT_lo[:, k, :], pair[bl], k == 0, k == KT - 1)
                    last.then_inc(unit_used, 1)
                    if j == 3 and not peeled:
                        pe.wait_ge(pair_free[1], i * 2 + b0)
                        turn_act()

            for g in range(8):
                wait_read(pe, ("hA", g))
            for n, n0, ug, ud, bgt, bd in ((FF_A, 0, U_GUA, U_DA, B_GUA, B_DA), (FF_B, FF_A, U_GUB, U_DB, B_GUB, B_DB)):
                gate_up(0, ug, bgt, n0, True)
                with pe.Fori(1, n) as i:
                    gate_up(i, ug, bgt, n0, False)
                def turn_last():
                    pe.wait_ge(pair_free[1], bd)
                    turn_act()

                def activations(b, k):
                    if b == 0 and k in (0, 4 * (n - 1)):
                        for q in range(2):
                            pe.wait_ge(ff_free[q], n0 + (n if k else n - 1))
                    return actT_hi[:, k, :], actT_lo[:, k, :]

                straight(ud, bd, 4, n * 4 // KU, activations, turn_last)

            def normed(b, k):
                if b == 0 and k in (0, 12):
                    for g in (range(6) if k == 0 else (6, 7)):
                        wait_read(pe, ("hB", g))
                return xT_hi[:, k, :], xT_lo[:, k, :]

            straight(U_PG, B_PG, 4, UPB, normed)

        @block.scalar
        def _(act):
            f = nc.scalar.activation
            act.wait_ge(masks_ready, 1)
            f(warm[:], half[:, 0:1], ACT.Square)
            act.dma_start(rows[0:KT, :], A["attn_norm"][0].rearrange("(k p) -> k p", p=P)).then_inc(rows_landed, 16)
            act.dma_start(rows[KT:2 * KT, :], A["ffn_norm"][0].rearrange("(k p) -> k p", p=P)).then_inc(rows_landed, 16)
            act.dma_start(rows[2 * KT:3 * KT, :], A["ple_norm"][0].rearrange("(k p) -> k p", p=P)).then_inc(rows_landed, 16)
            for i, n in enumerate(("gdn_norm", "q_norm", "k_norm")):
                act.dma_start(rows[3 * KT + i:3 * KT + i + 1, :], A[n]).then_inc(rows_landed, 16)

            def split(u, j):
                act.wait_ge(raw_landed[j % RING], (u - j % RING) * (16 // RING) + 16)
                if not isinstance(u, int) or u >= RING:
                    act.wait_ge(unit_used, u - (RING - 1))
                f(w_hi[j % RING][:], raw[j % RING][:], ACT.Copy).then_inc(hi_ready, 1)

            act.wait_ge(x_landed[0], 32)
            f(x_junk[:, :], h[:, 0, :], ACT.Square, accum_out=x_ss[:, 0:1]).then_inc(x_sq[0], 1)
            split(0, 0)
            act.wait_ge(x_rstd, 2)
            f(h[:, 0, :], h[:, 0, :], ACT.Copy, scale=x_rs[:, 0:1]).then_inc(x_scaled, 1)

            def post(step, b):
                bk, i, use_n = where((step, b))
                bh = heads(bk[:])
                c, hg = b % 2, b // 2
                ts = slice(c * P, c * P + P)
                B = G[c]
                hs = slice(HG * hg, HG * hg + HG)
                s = (step, b)
                if step == "gains":
                    wait_full(act, s)
                    f(gains[:, 0:NROW], bk[:, 0:NROW], ACT.Copy).then_inc(gain_s, 1)
                    read_out(s, f(gains[:, G_QS:G_QS + 1], bk[:, G_Q:G_Q + 1], ACT.Copy, scale=float(P) ** -0.5))
                    wait_read(act, s)
                    act.wait_ge(gain_s, 1)
                elif step in ("x", "hA", "hB"):
                    col = {"x": G_ATTN, "hA": G_FFN, "hB": G_PLE}[step]
                    wait_full(act, s)
                    for kk in range(2):
                        k = 2 * b + kk
                        f(xT_hi[:, k, :], bk[:, kk * TOK:(kk + 1) * TOK], ACT.Copy,
                          scale=gains[:, col + k:col + k + 1]).then_inc(x_hi, 1)
                elif step == "p":
                    wait_full(act, s)
                    f(pT_hi[:].rearrange("p k n -> p (k n)"), bk[:], ACT.Copy).then_inc(p_hi, 1)
                elif step == "baT":
                    wait_full(act, s)
                    read_out(s, f(baT[:], bk[0:2 * HEADS, 0:TOK], ACT.Copy))
                elif step == "ba":
                    wait_full(act, s)
                    f(sc["beta"][:], bk[:, 0:4 * HEADS].rearrange("p (t n) -> p t n", t=NT)[:, :, 0:HEADS],
                      ACT.Sigmoid).then_inc(beta_ready, 1)
                    act.wait_ge(small_landed, 48)
                    f(exp_a[:], a_log[:], ACT.Exp).then_inc(dt_act, 1)
                    act.wait_ge(dt_dve, 2)
                    f(sc["dt_exp"][:], sc["dt_abs"][:], ACT.Exp, scale=-1.0).then_inc(dt_act, 1)
                    act.wait_ge(dt_act, 2)
                    f(sc["dt_ln"][:], sc["dt_exp"][:], ACT.Ln, bias=1.0).then_inc(dt_act, 1)
                elif step == "gc":
                    wait_full(act, s)
                    f(sc["egc"][:], bk[:, 0:2 * HEADS].rearrange("p (t n) -> p t n", t=NT), ACT.Exp).then_inc(egc_ready, 1)
                elif step == "q_tok":
                    wait_full(act, s)
                    f(B["T"][:], bh, ACT.Square).then_inc(q_sq, 1)
                elif step == "k_tok":
                    wait_full(act, s)
                    f(B["TT"][:], bh, ACT.Square).then_inc(k_sq, 1)
                elif step == "qT":
                    wait_full(act, s)
                    read_out(s, f(ch[:, hs, ts], bh, ACT.Copy))
                elif step == "kT":
                    wait_full(act, s)
                    read_out(s, f(B["AT"][:], bh, ACT.Copy))
                elif step == "kbT":
                    wait_full(act, s)
                    read_out(s, f(ch[:, HEADS + HG * hg:HEADS + HG * hg + HG, ts], bh, ACT.Copy))
                elif step == "gcrow":
                    act.wait_ge(gap_ready, b + 1)
                    f(B["Y"][:], B["Y"][:], ACT.Exp).then_inc(exp_ready, 1)
                elif step == "T0":
                    wait_full(act, s)
                    act.wait_ge(kd_ready, b + 1)
                    read_out(s, f(B["T"][:], bh, ACT.Copy))
                elif step.startswith("TT"):
                    wait_full(act, s)
                    read_out(s, f(B["TT"][:], bh, ACT.Copy))
                elif step == "u":
                    wait_full(act, s)
                    read_out(s, f(B["T"][:], bh, ACT.Copy))
                elif step == "S":
                    wait_full(act, s)
                    read_out(s, f(state[:], bh, ACT.Copy))
                elif step == "o":
                    wait_read(act, s)
                    f(B["Y"][:], B["V"][:], ACT.Square).then_inc(o_sq, 1)
                elif step == "ogT":
                    wait_full(act, s)
                    f(og_hi[:, hs, ts], bh, ACT.Copy, scale=gains[:, G_GDN:G_GDN + 1]).then_inc(og_hi_ready, 1)
                elif step == "m_sq":
                    j = b // 2
                    wait_block(act, U_MIX + j * UPB + UPB - 1)
                    if b < 2:
                        wait_pair_read(act, B_MIX - 2 + c)
                    else:
                        act.wait_ge(m_sum, b - 1)
                    f(sq[c][:], pair[(B_MIX + j) % 2][c][:], ACT.Square).then_inc(m_sq, 1)
                elif step == "mT":
                    wait_full(act, s)
                    j = b // 2
                    col = G_QS if j < 2 else G_K
                    jh = j % 2
                    read_out(s, f(mT[j // 2][:, HG * jh:HG * jh + HG, ts], bh, ACT.Copy, scale=gains[:, col:col + 1]))
                elif step == "sc":
                    act.wait_ge(max_ready, 2 * (b + 1))
                    f(pr[c][:, 0:P], pr[c][:, 0:P], ACT.Exp, bias=nmax[c][:, 0:1],
                      accum_out=psum_p[c][:, 0:1]).then_inc(exp_done, 1)
                    f(pr[c][:, P:3 * P], pr[c][:, P:3 * P], ACT.Exp, bias=nmax[c][:, 1:2],
                      accum_out=psum_p[c][:, 1:2]).then_inc(exp_done, 1)
                elif step == "pT":
                    wait_full(act, s)
                    read_out(s, f(prT[c], bk[:, 0:3 * P], ACT.Copy))
                elif step == "pv":
                    wait_full(act, s)
                    f(om_hi[:, b, :], bk[:, 0:TOK], ACT.Copy).then_inc(om_hi_ready, 1)

            for n, s in enumerate(FIRST):
                post(*s)
                if n in (3, 6):
                    split(n // 3, n // 3)
            act.wait_ge(ba_landed, 16)
            f(wba_hi[:], wba_raw[:], ACT.Copy).then_inc(ba_hi, 1)

            def conv(i, bl, u, j):
                n = i * 2 + bl
                act.wait_ge(unit_used, n * UPB + (U_QKV + UPB))
                for m in range(4):
                    t0 = i * HEADS + (4 * bl + m)
                    act.wait_ge(small_landed, 48)
                    cs = slice(m % 2 * TOK, (m % 2 + 1) * TOK)
                    f(mn[m // 2][:, cs], pair[bl][m // 2][:, cs], ACT.Copy, scale=convw[:, bass.ds(t0 * CONV + (CONV - 1), 1)]).then_inc(tap3, 1)
                split(u, j)
                for q in range(2):
                    act.wait_ge(taps, n * 12 + (10 + 2 * q))
                    f(sq[q][:], mn[q][:], ACT.Sigmoid).then_inc(conv_sig, 1)

            act.wait_ge(small_landed, 48)

            def z_end(b):
                wait_block(act, (b + 1) * UPB - 1)
                if b:
                    wait_pair_read(act, b - 1)
                for t in range(NT):
                    f(sq[t][:], pair[b][t][:], ACT.Sigmoid).then_inc(z_sig, 1)

            def qkv(i, first):
                for j in range(2 * UPB):
                    if j % UPB:
                        split(i * (2 * UPB) + (U_QKV + j + LEAD), j + LEAD)
                    if first and j in (1, 5):
                        post("ba" if j == 1 else "gc", 0)
                    if j % UPB == UPB - 1:
                        if j >= UPB:
                            act.wait_ge(pair_free[0], i * 2 + 4)
                        else:
                            act.wait_ge(pair_free[1], i * 2 + 2)
                        conv(i, j // UPB, i * (2 * UPB) + (U_QKV + j + 1 + LEAD), j + 1 + LEAD)

            for u in range(2 * UPB):
                split(u + LEAD, u + LEAD)
                if (u + 1) % UPB == 0:
                    z_end(u // UPB)
            split(U_QKV + LEAD, LEAD)
            post("baT", 0)
            qkv(0, True)
            with act.Fori(1, 3) as i:
                qkv(i, False)

            def mix_end(b):
                wait_block(act, U_MIX + b * UPB + UPB - 1)
                n = B_MIX + b
                for t in range(NT):
                    f(mv[:, t, (b - 4) * CB:(b - 3) * CB], pair[n % 2][t][:], ACT.Copy).then_inc(pair_free[n % 2], 1)

            def res_end(last_unit, i, n):
                wait_block(act, last_unit)
                bno = (B_WO if i == 0 else B_DB) + n
                wait_pair_read(act, bno)
                for t in range(NT):
                    f(junk[:], h[:, t, n * CB:(n + 1) * CB], ACT.Square, accum_out=h_ss[i][:, t, n:n + 1]).then_inc(h_sq, 1)
                    act.wait_ge(h_sq, 8 * i + 2 * n + t + 1)

            for u in range(U_MIX, U_GUA):
                if u > U_MIX:
                    split(u + LEAD, u + LEAD)
                for k in range(2):
                    for s in AT[u][k]:
                        post(*s)
                if U_WO - 2 * UPB <= u < U_WO and (u + 1) % UPB == 0:
                    mix_end((u - U_MIX) // UPB)
                elif U_WO <= u < U_PP and (u + 1) % UPB == 0:
                    res_end(u, 0, (u - U_WO) // UPB)
                elif u >= U_PP:
                    wait_block(act, u)
                    n = u - U_PP
                    for t in range(NT):
                        f(pp[:, t, n * CB:(n + 1) * CB], pair[n % 2][t][:], ACT.Copy).then_inc(pair_free[n % 2], 1)

            act.wait_ge(h_rstd, 2)

            def turned(n, kt):
                for q in range(2):
                    act.wait_ge(ff_full[q], n + 1)
                    act.wait_ge(h_rstd, 2)
                    f(actT_hi[:, bass.ds(kt + 2 * q, 2), :], bg[q][:].rearrange("p (k n) -> p k n", k=2),
                      ACT.Copy).then_inc(act_hi_ready, 1)

            def gate_up(i, u0, b0, n0, peeled):
                for j in range(2 * UPB):
                    split(i * (2 * UPB) + (u0 + j + LEAD), j + LEAD)
                    if j == 3 and not peeled:
                        turned(i + (n0 - 1), i * 4 - 4)
                    if j == UPB - 1:
                        act.wait_ge(unit_used, i * (2 * UPB) + (u0 + UPB))
                        act.wait_ge(pair_free[1], i * 2 + b0)
                        for t in range(NT):
                            f(gate_s[t][:], pair[0][t][:], ACT.Sigmoid, scale=h_rs[0][:, t:t + 1]).then_inc(gate_sig, 1)

            for n, n0, ug, ud, bgt in ((FF_A, 0, U_GUA, U_DA, B_GUA), (FF_B, FF_A, U_GUB, U_DB, B_GUB)):
                gate_up(0, ug, bgt, n0, True)
                with act.Fori(1, n) as i:
                    gate_up(i, ug, bgt, n0, False)
                per = n * 4 // KU
                if n0 == 0:
                    for j in range(4 * per):
                        split(ud + j + LEAD, j + LEAD)
                        if j == 3:
                            turned(n0 + n - 1, 4 * (n - 1))
                else:
                    for j in range(4 * per):
                        split(ud + j + LEAD, j + LEAD)
                        if j == 3:
                            turned(n0 + n - 1, 4 * (n - 1))
                        for k in range(2):
                            for s in AT[ud + j][k]:
                                post(*s)
                        if (j + 1) % per == 0:
                            res_end(ud + j, 1, j // per)
            for u in range(U_PG, UNITS):
                if u + LEAD < UNITS:
                    split(u + LEAD, u + LEAD)
                for k in range(2):
                    for s in AT[u][k]:
                        post(*s)
                if u == U_PG + 4:
                    act.wait_ge(h_rstd, 4)
                if (u - U_PG + 1) % UPB == 0:
                    b = (u - U_PG) // UPB
                    wait_block(act, u)
                    if b:
                        act.wait_ge(out_ready, 2 * b)
                    for t in range(NT):
                        f(gate_s[t][:], pair[b % 2][t][:], ACT.Sigmoid, scale=h_rs[1][:, t:t + 1]).then_inc(pair_free[b % 2], 1)

        @block.vector
        def _(dve):
            v = nc.vector

            def split(u, j):
                dve.wait_ge(hi_ready, u + 1)
                v.tensor_tensor(w_lo[j % RING][:], raw[j % RING][:], w_hi[j % RING][:].bitcast(F32),
                                ALU.subtract).then_inc(lo_ready, 1)

            hi_base = {"x": 0, "hA": KT, "hB": 2 * KT}

            def post(step, b):
                bk, i, use_n = where((step, b))
                bh = heads(bk[:])
                c, hg = b % 2, b // 2
                ts = slice(c * P, c * P + P)
                B = G[c]
                hs = slice(HG * hg, HG * hg + HG)
                s = (step, b)
                if step in ("x", "hA", "hB"):
                    col = {"x": G_ATTN, "hA": G_FFN, "hB": G_PLE}[step]
                    dve.wait_ge(x_hi, hi_base[step] + 2 * b + 2)
                    for kk in range(2):
                        k = 2 * b + kk
                        m = v.scalar_tensor_tensor(out=xT_lo[:, k, :], in0=bk[:, kk * TOK:(kk + 1) * TOK],
                                                   scalar=gains[:, col + k:col + k + 1],
                                                   in1=xT_hi[:, k, :].bitcast(F32), op0=ALU.mult, op1=ALU.subtract)
                    read_out(s, m)
                elif step == "p":
                    dve.wait_ge(p_hi, 1)
                    read_out(s, v.tensor_tensor(pT_lo[:].rearrange("p k n -> p (k n)"), bk[:],
                                                pT_hi[:].rearrange("p k n -> p (k n)").bitcast(F32), ALU.subtract))
                elif step == "ba":
                    dve.wait_ge(consts_ready, 2)
                    dve.wait_ge(beta_ready, 1)
                    dve.wait_ge(small_landed, 48)
                    read_out(s, v.tensor_tensor(
                        sc["dt_in"][:], bk[:, 0:4 * HEADS].rearrange("p (t n) -> p t n", t=NT)[:, :, HEADS:2 * HEADS],
                        dt_b[:].unsqueeze(1).to_broadcast([P, NT, HEADS]), ALU.add))
                    wait_read(dve, s)
                    v.tensor_scalar(sc["dt_sum"][:], sc["dt_in"][:], 0.0, None, ALU.max).then_inc(dt_dve, 1)
                    dve.wait_ge(dt_dve, 1)
                    v.scalar_tensor_tensor(out=sc["dt_abs"][:], in0=sc["dt_sum"][:], scalar=2.0, in1=sc["dt_in"][:],
                                           op0=ALU.mult, op1=ALU.subtract).then_inc(dt_dve, 1)
                    dve.wait_ge(dt_act, 3)
                    v.tensor_tensor(sc["dt_sum"][:], sc["dt_sum"][:], sc["dt_ln"][:], ALU.add).then_inc(dt_dve, 1)
                    dve.wait_ge(dt_dve, 3)
                    v.scalar_tensor_tensor(out=sc["g"][:], in0=sc["dt_sum"][:], scalar=-1.0,
                                           in1=exp_a[:].unsqueeze(1).to_broadcast([P, NT, HEADS]),
                                           op0=ALU.mult, op1=ALU.mult).then_inc(g_ready, 1)
                elif step == "gc":
                    dve.wait_ge(egc_ready, 1)
                    read_out(s, v.tensor_copy(sc["gc"][:], bk[:, 0:2 * HEADS].rearrange("p (t n) -> p t n", t=NT)))
                elif step == "q_tok":
                    dve.wait_ge(q_sq, b + 1)
                    v.reduce_sum(q_ss[c][:], B["T"][:], AX_X).then_inc(q_sum, 1)
                elif step == "q_n":
                    dve.wait_ge(q_rstd, 2 * (b + 1))
                    read_out(s, v.tensor_tensor(B["Y"][:], bh, over_cols(q_rs[c][:]), ALU.mult))
                elif step == "k_tok":
                    dve.wait_ge(k_sq, b + 1)
                    v.reduce_sum(k_ss[c][:], B["TT"][:], AX_X).then_inc(k_sum, 1)
                elif step == "k_n":
                    dve.wait_ge(k_rstd, 2 * (b + 1))
                    read_out(s, v.tensor_tensor(B["T"][:], bh, over_cols(k_rs[c][:]), ALU.mult))
                elif step == "v_tok":
                    wait_full(dve, s)
                    read_out(s, v.tensor_tensor(B["V"][:], bh, over_cols(sc["beta"][:, c, hs]), ALU.mult))
                elif step == "gcrow":
                    wait_full(dve, s)
                    wait_read(dve, ("gc", 0))
                    v.tensor_tensor(B["Y"][:], bh, over_cols(sc["gc"][:, c, hs]), ALU.subtract).then_inc(bank_free[i], 1)
                    wait_read(dve, s)
                    v.tensor_scalar(B["Y"][:], B["Y"][:], 0.0, None, ALU.min).then_inc(gap_ready, 1)
                elif step == "gramQ":
                    wait_full(dve, s)
                    dve.wait_ge(decay_ready, b + 1)
                    read_out(s, v.tensor_tensor(ch[:, 2 * HEADS + HG * hg:2 * HEADS + HG * hg + HG, ts], bh, B["Y"][:],
                                                ALU.mult))
                elif step == "gramA":
                    wait_full(dve, s)
                    read_out(s, v.tensor_tensor(B["AT"][:], bh, B["Y"][:], ALU.mult))
                    wait_read(dve, s)
                    v.tensor_tensor(B["Y"][:], B["AT"][:], over_heads(join0T[:]), ALU.mult).then_inc(tt_mid, 1)
                    dve.wait_ge(tt_mid, b + 1)
                    v.tensor_tensor(B["TT"][:], over_heads(ident[:]), B["Y"][:], ALU.subtract).then_inc(tt0, 1)
                elif step[0] == "Y":
                    wait_full(dve, s)
                    read_out(s, v.tensor_tensor(B["Y"][:], bh, over_heads(join[:, int(step[1:]), :]), ALU.mult))
                elif step == "ZT":
                    wait_full(dve, s)
                    read_out(s, v.tensor_tensor(B["TT"][:], B["TT"][:], bh, ALU.subtract))
                elif step[0] == "Z":
                    wait_full(dve, s)
                    read_out(s, v.tensor_tensor(B["T"][:], B["T"][:], bh, ALU.subtract))
                elif step == "ks":
                    wait_full(dve, s)
                    read_out(s, v.tensor_tensor(B["Y"][:], bh, over_cols(sc["egc"][:, c, hs]), ALU.mult))
                    wait_read(dve, s)
                    v.tensor_tensor(B["V"][:], B["V"][:], B["Y"][:], ALU.subtract).then_inc(r_ready, 1)
                elif step == "qs":
                    wait_full(dve, s)
                    dve.wait_ge(r_ready, (b + 1) // 2)
                    read_out(s, v.tensor_tensor(B["Y"][:], bh, over_cols(sc["egc"][:, c, hs]), ALU.mult))
                elif step == "o":
                    wait_full(dve, s)
                    if c:
                        wait_read(dve, ("qs", b))
                        read_out(s, v.tensor_tensor(B["V"][:], bh, B["Y"][:], ALU.add))
                    else:
                        read_out(s, v.tensor_copy(B["V"][:], bh))
                elif step == "o_s":
                    dve.wait_ge(o_sq, b + 1)
                    v.reduce_sum(o_ss[c][:], B["Y"][:], AX_X).then_inc(o_sum, 1)
                elif step == "o_n":
                    dve.wait_ge(o_rstd, 2 * (b + 1))
                    v.tensor_tensor(B["V"][:], B["V"][:], over_cols(o_rs[c][:]), ALU.mult).then_inc(o_scaled, 1)
                    dve.wait_ge(o_scaled, b + 1)
                    wait_pair_read(dve, hg)
                    v.tensor_tensor(B["V"][:], B["V"][:], heads(zg[:, c, hg * CB:(hg + 1) * CB]), ALU.mult).then_inc(og_ready, 1)
                elif step == "m_sq":
                    n = B_MIX + b // 2
                    dve.wait_ge(m_sq, b + 1)
                    if b >= 2:
                        wait_full(dve, ("mT", b - 2))
                    v.tensor_copy(mn[c][:], pair[n % 2][c][:]).then_inc(pair_free[n % 2], 1)
                    v.reduce_sum(m_ss[c][:], heads(sq[c][:]), AX_X).then_inc(m_sum, 1)
                elif step == "m_n":
                    wait_pair_read(dve, B_MIX + b // 2)
                    dve.wait_ge(m_rstd, 2 * (b + 1))
                    v.tensor_tensor(heads(mn[c][:]), heads(mn[c][:]), over_cols(m_rs[c][:]), ALU.mult).then_inc(mn_ready, 1)
                elif step == "ogT":
                    dve.wait_ge(og_hi_ready, b + 1)
                    for j in range(HG):
                        hd = HG * hg + j
                        m = v.scalar_tensor_tensor(out=og_lo[:, hd, ts], in0=bh[:, j, :], scalar=gains[:, G_GDN:G_GDN + 1],
                                                   in1=og_hi[:, hd, ts].bitcast(F32), op0=ALU.mult, op1=ALU.subtract)
                    read_out(s, m)
                elif step == "sc":
                    wait_full(dve, s)
                    if b >= 2:
                        wait_full(dve, ("pT", b - 2))
                    read_out(s, v.tensor_tensor(pr[c][:], bk[:, 0:3 * P], causal[:], ALU.add))
                    wait_read(dve, s)
                    for q, (lo, up) in enumerate(((0, P), (P, 3 * P))):
                        v.tensor_reduce(nmax[c][:, q:q + 1], pr[c][:, lo:up], AX_X, ALU.max, negate=True).then_inc(max_ready, 1)
                    dve.wait_ge(exp_done, 2 * (b + 1))
                    v.reciprocal(rsum[c][:], psum_p[c][:]).then_inc(rsum_ready, 1)
                    dve.wait_ge(rsum_ready, b + 1)
                    v.tensor_scalar(pr[c][:, 0:P], pr[c][:, 0:P], rsum[c][:, 0:1], None, ALU.mult)
                    v.tensor_scalar(pr[c][:, P:3 * P], pr[c][:, P:3 * P], rsum[c][:, 1:2], None, ALU.mult).then_inc(p_ready, 1)
                elif step == "pv":
                    dve.wait_ge(om_hi_ready, b + 1)
                    read_out(s, v.tensor_tensor(om_lo[:, b, :], bk[:, 0:TOK], om_hi[:, b, :].bitcast(F32), ALU.subtract))

            dve.wait_ge(x_landed[1], 32)
            v.tensor_tensor_reduce(x_junk2[:], h[:, 1, :], h[:, 1, :], 1.0, 0.0, ALU.mult, ALU.add,
                                   x_ss[:, 1:2]).then_inc(x_sq[1], 1)
            split(0, 0)
            dve.wait_ge(x_rstd, 4)
            v.tensor_scalar(h[:, 1, :], h[:, 1, :], x_rs[:, 1:2], None, ALU.mult).then_inc(x_scaled, 1)
            for n, s in enumerate(FIRST):
                post(*s)
                if n in (3, 6):
                    split(n // 3, n // 3)
            dve.wait_ge(ba_hi, 1)
            v.tensor_tensor(wba_lo[:], wba_raw[:], wba_hi[:].bitcast(F32), ALU.subtract).then_inc(ba_lo, 1)

            dve.wait_ge(small_landed, 48)

            def conv(i, bl, u, j):
                n = i * 2 + bl
                done = 0
                for tap in (2, 1, 0):
                    if tap == 0:
                        split(u, j)
                    sh = CONV - 1 - tap
                    for m in range(4):
                        t0 = i * HEADS + (4 * bl + m)
                        if tap == 2:
                            dve.wait_ge(tap3, n * 4 + (m // 2 * 2 + 2))
                        else:
                            dve.wait_ge(taps, n * 12 + (done - 3))
                        o = mn[m // 2][:, m % 2 * TOK + sh:(m % 2 + 1) * TOK]
                        src = pair[bl][m // 2][:, m % 2 * TOK:(m % 2 + 1) * TOK - sh]
                        v.scalar_tensor_tensor(out=o, in0=src, scalar=convw[:, bass.ds(t0 * CONV + tap, 1)], in1=o,
                                               op0=ALU.mult, op1=ALU.add).then_inc(taps, 1)
                        done += 1
                for q in range(2):
                    dve.wait_ge(conv_sig, n * 2 + (q + 1))
                    t0 = i * HEADS + (4 * bl + 2 * q)
                    v.tensor_tensor(ch[:, bass.ds(t0, 2), :], mn[q][:].rearrange("p (m n) -> p m n", m=2),
                                    sq[q][:].rearrange("p (m n) -> p m n", m=2), ALU.mult).then_inc(pair_free[bl], 1)

            def qkv(i, first):
                for j in range(2 * UPB):
                    if j % UPB:
                        split(i * (2 * UPB) + (U_QKV + j + LEAD), j + LEAD)
                    if first and j in (1, 5):
                        post("ba" if j == 1 else "gc", 0)
                    if j % UPB == UPB - 1:
                        conv(i, j // UPB, i * (2 * UPB) + (U_QKV + j + 1 + LEAD), j + 1 + LEAD)

            for u in range(2 * UPB):
                split(u + LEAD, u + LEAD)
                if (u + 1) % UPB == 0:
                    b = u // UPB
                    for t in range(NT):
                        dve.wait_ge(z_sig, 2 * b + t + 1)
                        v.tensor_tensor(zg[:, t, b * CB:(b + 1) * CB], pair[b][t][:], sq[t][:],
                                        ALU.mult).then_inc(pair_free[b], 1)
            split(U_QKV + LEAD, LEAD)
            qkv(0, True)
            with dve.Fori(1, 3) as i:
                qkv(i, False)

            def res_end(last_unit, i, n):
                wait_block(dve, last_unit)
                bno = (B_WO if i == 0 else B_DB) + n
                if i == 0:
                    dve.wait_ge(x_again[n], 16)
                for t in range(NT):
                    o = h[:, t, n * CB:(n + 1) * CB]
                    v.tensor_tensor(o, o, pair[bno % 2][t][:], ALU.add).then_inc(pair_free[bno % 2], 1)
                if n == 3:
                    dve.wait_ge(h_sq, 8 * (i + 1))
                    v.reduce_sum(h_s[i][:], h_ss[i][:], AX_X).then_inc(h_sum, 1)

            for u in range(U_MIX, U_GUA):
                if u > U_MIX:
                    split(u + LEAD, u + LEAD)
                for k in range(2):
                    for s in AT[u][k]:
                        post(*s)
                if U_WO <= u < U_PP and (u + 1) % UPB == 0:
                    res_end(u, 0, (u - U_WO) // UPB)

            dve.wait_ge(h_rstd, 2)

            def turned(n, kt):
                for q in range(2):
                    dve.wait_ge(act_hi_ready, n * 2 + (q + 1))
                    ks = bass.ds(kt + 2 * q, 2)
                    v.tensor_tensor(actT_lo[:, ks, :], bg[q][:].rearrange("p (k n) -> p k n", k=2),
                                    actT_hi[:, ks, :].bitcast(F32), ALU.subtract).then_inc(ff_free[q], 1)

            def gate_up(i, u0, b0, n0, peeled):
                for j in range(2 * UPB):
                    split(i * (2 * UPB) + (u0 + j + LEAD), j + LEAD)
                    if j == 3 and not peeled:
                        turned(i + (n0 - 1), i * 4 - 4)
                    if j == UPB - 1:
                        for t in range(NT):
                            dve.wait_ge(gate_sig, i * 2 + (2 * n0 + t + 1))
                            v.scalar_tensor_tensor(out=gate_s[t][:], in0=pair[0][t][:], scalar=h_rs[0][:, t:t + 1],
                                                   in1=gate_s[t][:], op0=ALU.mult, op1=ALU.mult).then_inc(pair_free[0], 1)
                    if j == 2 * UPB - 1:
                        dve.wait_ge(unit_used, i * (2 * UPB) + (u0 + 2 * UPB))
                        dve.wait_ge(pair_free[0], i * 2 + (b0 + 2))
                        for t in range(NT):
                            v.scalar_tensor_tensor(out=act_s[t][:], in0=pair[1][t][:], scalar=h_rs[0][:, t:t + 1],
                                                   in1=gate_s[t][:], op0=ALU.mult, op1=ALU.mult).then_inc(pair_free[1], 1)

            for n, n0, ug, ud, bgt in ((FF_A, 0, U_GUA, U_DA, B_GUA), (FF_B, FF_A, U_GUB, U_DB, B_GUB)):
                gate_up(0, ug, bgt, n0, True)
                with dve.Fori(1, n) as i:
                    gate_up(i, ug, bgt, n0, False)
                per = n * 4 // KU
                if n0 == 0:
                    for j in range(4 * per):
                        split(ud + j + LEAD, j + LEAD)
                        if j == 3:
                            turned(n0 + n - 1, 4 * (n - 1))
                        if (j + 1) % per == 0:
                            b = j // per
                            wait_block(dve, ud + j)
                            for t in range(NT):
                                o = h[:, t, b * CB:(b + 1) * CB]
                                v.tensor_tensor(o, o, pair[b % 2][t][:], ALU.add).then_inc(pair_free[b % 2], 1)
                else:
                    for j in range(4 * per):
                        split(ud + j + LEAD, j + LEAD)
                        if j == 3:
                            turned(n0 + n - 1, 4 * (n - 1))
                        for k in range(2):
                            for s in AT[ud + j][k]:
                                post(*s)
                        if (j + 1) % per == 0:
                            res_end(ud + j, 1, j // per)
            for u in range(U_PG, UNITS):
                if u + LEAD < UNITS:
                    split(u + LEAD, u + LEAD)
                for k in range(2):
                    for s in AT[u][k]:
                        post(*s)
                if (u - U_PG + 1) % UPB == 0:
                    b = (u - U_PG) // UPB
                    cs = slice(b * CB, b * CB + CB)
                    n = B_PG + b
                    for t in range(NT):
                        dve.wait_ge(pair_free[n % 2], 2 * (n // 2) + t + 1)
                        v.tensor_tensor(gate_s[t][:], gate_s[t][:], pp[:, t, cs], ALU.mult).then_inc(pg_mul, 1)
                        dve.wait_ge(pg_mul, 2 * b + t + 1)
                        v.tensor_tensor(h[:, t, cs], h[:, t, cs], gate_s[t][:], ALU.add).then_inc(out_ready, 1)


_INS = ["x", "p", "attn_norm", "w_in", "conv_w", "A_log", "dt_bias", "gdn_norm", "q_norm", "k_norm",
        "w_o", "ffn_norm", "w_gate", "w_up", "w_down", "ple_norm", "w_ple_gate", "w_ple_proj"]


def kernel(**inputs):
    import numpy as _np
    import concourse.bacc as _bacc
    from concourse import mybir as _mybir
    from concourse.bass_utils import run_bass_kernel_spmd as _run

    nc = _bacc.Bacc("TRN2", target_bir_lowering=False, num_devices=1)
    arrays, args = {}, {}
    for name in _INS:
        a = _np.ascontiguousarray(inputs[name])
        arrays[f"in_{name}_dram"] = a
        args[name] = nc.dram_tensor(f"in_{name}_dram", a.shape, _mybir.dt.from_np(a.dtype), kind="ExternalInput").ap()
    args["out"] = nc.dram_tensor("out_0_dram", (1, TOK, D), _mybir.dt.float32, kind="ExternalOutput").ap()
    build(nc, args)
    r = _run(nc, [arrays], core_ids=[0])
    return r.results[0]["out_0_dram"]
```
